# Optimizing a Trainium2 kernel written in Bass

```python
import jax, jax.numpy as jnp
from jax import lax
import numpy as np

D_MODEL = 1024
BATCH = 1
SEQ = 2048
DEPTH = 1

D_MIX = D_MODEL
D_POOL = D_MIX // 2
POOL_WINDOWS = (2, 4, 8, 16)
N_POOL_GROUPS = len(POOL_WINDOWS)
POOL_GROUP = D_POOL // N_POOL_GROUPS
D_CONV = D_MIX - D_POOL
CONV_WIDTH = 3
D_PROJ = D_POOL + 3 * D_CONV

N_EXPERTS = 16
N_EXPERT_GROUPS = 4
EXPERTS_PER_GROUP = N_EXPERTS // N_EXPERT_GROUPS
TOP_K = 2
D_EXPERT = D_MODEL // 2
EXPERT_BLOCK = 128

ALPHA = float((2 * DEPTH) ** 0.25)
BETA = float((8 * DEPTH) ** -0.25)
LN_EPS = 1e-5

kernel_name = "hybrid_pool_conv_grouped_moe_deepnorm"

def layer_norm(x, g, b):
    xf = x.astype(jnp.float32)
    mu = jnp.mean(xf, axis=-1, keepdims=True)
    xc = xf - mu
    var = jnp.mean(xc * xc, axis=-1, keepdims=True)
    return (xc * lax.rsqrt(var + LN_EPS) * g + b).astype(x.dtype)

def causal_multiscale_pool(v, pool_w, pool_scale):
    bsz, s, _ = v.shape
    vf = v.astype(jnp.float32)
    csum = jnp.cumsum(vf, axis=1)
    n_avail = jnp.arange(1, s + 1, dtype=jnp.float32)
    outs = []
    for g, win in enumerate(POOL_WINDOWS):
        sl = slice(g * POOL_GROUP, (g + 1) * POOL_GROUP)
        cg = csum[..., sl]
        prev = jnp.pad(cg, ((0, 0), (win, 0), (0, 0)))[:, :s]
        mean = (cg - prev) / jnp.minimum(n_avail, float(win))[None, :, None]
        outs.append(mean - vf[..., sl])
    pooled = jnp.stack(outs, axis=2).astype(v.dtype)
    mixed = jnp.einsum("bsgc,gcd->bsgd", pooled, pool_w).reshape(bsz, s, D_POOL)
    return mixed * pool_scale

def gated_short_conv(gate_b, gate_c, u, conv_w, conv_b):
    z = gate_c * u
    y = lax.conv_general_dilated(
        z, conv_w[:, None, :], window_strides=(1,), padding=[(CONV_WIDTH - 1, 0)],
        dimension_numbers=("NWC", "WIO", "NWC"), feature_group_count=D_CONV)
    return gate_b * (y + conv_b)

def hybrid_mixer(h, w_in, pool_w, pool_scale, conv_w, conv_b, w_out):
    proj = h @ w_in
    v = proj[..., :D_POOL]
    gb = proj[..., D_POOL:D_POOL + D_CONV]
    gc = proj[..., D_POOL + D_CONV:D_POOL + 2 * D_CONV]
    u = proj[..., D_POOL + 2 * D_CONV:]
    pool_out = causal_multiscale_pool(v, pool_w, pool_scale)
    conv_out = gated_short_conv(gb, gc, u, conv_w, conv_b)
    return jnp.concatenate([pool_out, conv_out], axis=-1) @ w_out

def grouped_moe(x, w_router, router_bias, w1, w3, w2):
    t, d = x.shape
    probs = jax.nn.softmax((x @ w_router).astype(jnp.float32), axis=-1)
    sel = probs + router_bias.astype(jnp.float32)
    grp_score = lax.top_k(sel.reshape(t, N_EXPERT_GROUPS, EXPERTS_PER_GROUP), 2)[0].sum(-1)
    gidx = jnp.argmax(grp_score, axis=-1)
    gmask = jnp.arange(N_EXPERT_GROUPS)[None, :] == gidx[:, None]
    emask = jnp.repeat(gmask, EXPERTS_PER_GROUP, axis=1)
    _, eidx = lax.top_k(jnp.where(emask, sel, -jnp.inf), TOP_K)
    gate = jnp.take_along_axis(probs, eidx, axis=-1)
    gate = gate / jnp.sum(gate, axis=-1, keepdims=True)

    m = t * TOP_K
    flat_e = eidx.reshape(m).astype(jnp.int32)
    flat_tok = jnp.arange(m, dtype=jnp.int32) // TOP_K
    order = jnp.argsort(flat_e, stable=True)
    e_sorted = flat_e[order]
    counts = jnp.bincount(flat_e, length=N_EXPERTS)
    starts = jnp.cumsum(counts) - counts
    padded = ((counts + EXPERT_BLOCK - 1) // EXPERT_BLOCK) * EXPERT_BLOCK
    pend = jnp.cumsum(padded)
    pstarts = pend - padded
    rank = jnp.arange(m, dtype=jnp.int32) - starts[e_sorted]
    dest_sorted = (pstarts[e_sorted] + rank).astype(jnp.int32)
    dest = jnp.zeros((m,), jnp.int32).at[order].set(dest_sorted)
    n_rows = ((m + EXPERT_BLOCK - 1) // EXPERT_BLOCK + N_EXPERTS) * EXPERT_BLOCK
    n_blocks = n_rows // EXPERT_BLOCK
    xbuf = jnp.zeros((n_rows, d), x.dtype).at[dest].set(x[flat_tok])
    blk_start = jnp.arange(n_blocks, dtype=jnp.int32) * EXPERT_BLOCK
    blk_e = jnp.minimum(jnp.searchsorted(pend, blk_start, side="right"), N_EXPERTS - 1)

    def expert_block(args):
        xb, e = args
        hid = jax.nn.silu(xb @ w1[e]) * (xb @ w3[e])
        return hid @ w2[e]

    ybuf = lax.map(expert_block, (xbuf.reshape(n_blocks, EXPERT_BLOCK, d), blk_e))
    ybuf = ybuf.reshape(n_rows, d)
    y = ybuf[dest].reshape(t, TOP_K, d) * gate[..., None].astype(x.dtype)
    return jnp.sum(y, axis=1)

def setup_inputs(seed: int = 0) -> dict:
    key = jax.random.key(seed)
    ks = jax.random.split(key, 20)
    f32 = jnp.float32
    nrm = lambda k, shape: jax.random.normal(k, shape, f32)
    return {
        "x": nrm(ks[0], (BATCH, SEQ, D_MODEL)),
        "ln_in_g": 1.0 + 0.02 * nrm(ks[1], (D_MODEL,)),
        "ln_in_b": 0.02 * nrm(ks[2], (D_MODEL,)),
        "w_in": nrm(ks[3], (DEPTH, D_MODEL, D_PROJ)) * D_MODEL ** -0.5,
        "pool_w": nrm(ks[4], (DEPTH, N_POOL_GROUPS, POOL_GROUP, POOL_GROUP)) * POOL_GROUP ** -0.5,
        "pool_scale": 1.0 + 0.1 * nrm(ks[5], (DEPTH, D_POOL)),
        "conv_w": nrm(ks[6], (DEPTH, CONV_WIDTH, D_CONV)) * CONV_WIDTH ** -0.5,
        "conv_b": 0.02 * nrm(ks[7], (DEPTH, D_CONV)),
        "w_out": nrm(ks[8], (DEPTH, D_MIX, D_MODEL)) * (D_MIX ** -0.5 * BETA),
        "ln1_g": 1.0 + 0.02 * nrm(ks[9], (DEPTH, D_MODEL)),
        "ln1_b": 0.02 * nrm(ks[10], (DEPTH, D_MODEL)),
        "w_router": nrm(ks[11], (D_MODEL, N_EXPERTS)) * D_MODEL ** -0.5,
        "router_bias": 0.01 * nrm(ks[12], (N_EXPERTS,)),
        "exp_w1": nrm(ks[13], (DEPTH, N_EXPERTS, D_MODEL, D_EXPERT)) * D_MODEL ** -0.5,
        "exp_w3": nrm(ks[14], (DEPTH, N_EXPERTS, D_MODEL, D_EXPERT)) * D_MODEL ** -0.5,
        "exp_w2": nrm(ks[15], (DEPTH, N_EXPERTS, D_EXPERT, D_MODEL)) * (D_EXPERT ** -0.5 * BETA),
        "ln2_g": 1.0 + 0.02 * nrm(ks[16], (DEPTH, D_MODEL)),
        "ln2_b": 0.02 * nrm(ks[17], (DEPTH, D_MODEL)),
    }

def reference(x, ln_in_g, ln_in_b, w_in, pool_w, pool_scale, conv_w, conv_b, w_out,
              ln1_g, ln1_b, w_router, router_bias, exp_w1, exp_w3, exp_w2, ln2_g, ln2_b):
    bsz, s, d = x.shape
    h = layer_norm(x, ln_in_g, ln_in_b)
    for l in range(DEPTH):
        mix = hybrid_mixer(h, w_in[l], pool_w[l], pool_scale[l], conv_w[l], conv_b[l], w_out[l])
        h = layer_norm(ALPHA * h + mix, ln1_g[l], ln1_b[l])
        ffn = grouped_moe(h.reshape(bsz * s, d), w_router, router_bias,
                          exp_w1[l], exp_w3[l], exp_w2[l]).reshape(bsz, s, d)
        h = layer_norm(ALPHA * h + ffn, ln2_g[l], ln2_b[l])
    return h


_drawn_inputs = setup_inputs


def setup_inputs(seed=0):
    import zlib

    import numpy as np

    out = dict(_drawn_inputs(seed))
    spreads = {}
    factors = {}
    for name, (base, spread) in spreads.items():
        noise = np.random.default_rng([zlib.crc32(name.encode()), seed]).standard_normal(out[name].shape)
        drawn = base * np.exp(spread * noise) if base else spread * noise
        out[name] = __import__('jax').numpy.asarray(drawn.astype(out[name].dtype))
    for name, factor in factors.items():
        out[name] = (out[name] * factor).astype(out[name].dtype)
    return out
```

```python
from contextlib import ExitStack

import numpy as np

import concourse.bass as bass
import concourse.mybir as mybir

F32 = mybir.dt.float32
F32R = mybir.dt.float32r
I32 = mybir.dt.int32
U32 = mybir.dt.uint32
ACT = mybir.ActivationFunctionType
ALU = mybir.AluOpType
AX = mybir.AxisListType

P = 128
SEQ = 2048
D = 1024
KT = D // P
CHUNK = 512
NCH = SEQ // CHUNK
TPC = CHUNK // P
NT = SEQ // P
WINDOWS = (2, 4, 8, 16)
NG = len(WINDOWS)
HIST = 16
CONV_W = 3
NE = 16
NEG = 4
EPG = NE // NEG
DE = 512
FT = DE // P
ALPHA = float(2.0 ** 0.25)
EPS = 1e-5
UNIT = 2048
RING = 8
RING1 = 4
CU = 12
EU = 6
MU = NCH * CU
NB = 48
NBP = NB + 1
OOB = 65536.0
BIG = 1.0e30
DVE_PER_CHUNK = 62


class Chain:

    def __init__(self, eng, sem):
        self.eng, self.sem, self.n, self.turn, self.per = eng, sem, 0, None, 0

    def mark(self, ins):
        ins.then_inc(self.sem, 1)
        self.n += 1
        return self.n if self.turn is None else self.turn * self.per + self.n

    def need(self, value):
        self.eng.wait_ge(self.sem, value)

    def link(self, ins):
        self.need(self.mark(ins))

    def enter(self, turn, per):
        self.turn, self.per, self.at = turn, per, self.n

    def leave(self, turns):
        assert self.n - self.at == self.per, (self.n - self.at, self.per)
        self.turn, self.n = None, self.at + turns * self.per


def carry(eng, sem):
    eng.sem_inc(sem, 1)


def build(nc, x, ln_in_g, ln_in_b, w_in, pool_w, pool_scale, conv_w, conv_b, w_out, ln1_g, ln1_b,
          w_router, router_bias, exp_w1, exp_w3, exp_w2, ln2_g, ln2_b, out):
    h0_dram = nc.dram_tensor("h0_scratch", (SEQ, D), F32).ap()
    h1_dram = nc.dram_tensor("h1_scratch", (SEQ, D), F32).ap()
    y_dram = nc.dram_tensor("y_scratch", (2 * SEQ, D), F32).ap()

    x_rows, out_rows = x[0], out[0]
    w_in_v = w_in[0].rearrange("(k p) (s g c) -> p k s g c", p=P, s=4, g=NG)
    w_out_v = w_out[0].rearrange("(a b r p) (n c) -> p b n a r c", p=P, a=2, b=2, n=2)
    w1_v = exp_w1[0].rearrange("e (k p) f -> e p k f", p=P)
    w3_v = exp_w3[0].rearrange("e (k p) f -> e p k f", p=P)
    w2_v = exp_w2[0].rearrange("e (k p) n -> e p k n", p=P)

    with ExitStack() as ctx:
        def sb(name, shape, dt=F32):
            return ctx.enter_context(nc.sbuf_tensor(name, shape, dt))

        def sem(name):
            return ctx.enter_context(nc.semaphore(name))

        ring_hi = sb("ring_hi", [P, RING, UNIT], F32R)
        ring_lo = sb("ring_lo", [P, RING, UNIT], F32R)
        stage = sb("stage", [P, 2, UNIT])
        ident = sb("ident", [P, P])
        gate = sb("gate", [P, NBP])
        gat_idx = sb("gat_idx", [P, NBP], U32)
        put_idx = sb("put_idx", [P, NBP], U32)
        gat_now = sb("gat_now", [P, 1], U32)
        put_now = sb("put_now", [P, 1], U32)
        table = sb("table", [P, 4, NBP], I32)
        nblocks = sb("nblocks", [P, 1], I32)
        half = sb("half", [P, 1])
        arena = sb("arena", [P, 15360])
        arena_at = nc.sbuf_base - 4 * 15360
        arena_at = (arena_at + 31) // 32 * 32

        class Place:
            def __init__(self):
                self.at = arena_at

            def __call__(self, name, shape, dt=F32):
                t = nc.alloc_sbuf_tensor_at(name, shape, dt, offset=self.at)
                self.at += 4 * int(np.prod(shape[1:]))
                self.at = (self.at + 31) // 32 * 32
                assert self.at <= arena_at + 4 * 15360, (name, self.at - arena_at)
                return t

        m = Place()
        g_in = m("g_in", [P, D])
        b_in = m("b_in", [P, D])
        g_1 = m("g_1", [P, D])
        b_1 = m("b_1", [P, D])
        hrow = m("hrow", [P, 2, D])
        hres = m("hres", [P, TPC, D])
        h1t = m("h1t", [P, KT, P])
        vext = m("vext", [P, HIST + CHUNK])
        sum_a = m("sum_a", [P, HIST + CHUNK])
        sum_b = m("sum_b", [P, HIST + CHUNK])
        zext = m("zext", [P, CONV_W - 1 + CHUNK])
        cacc = m("cacc", [P, CHUNK])
        pw_hi = m("pw_hi", [P, NG, P], F32R)
        pw_lo = m("pw_lo", [P, NG, P], F32R)
        vhist = m("vhist", [P, NG, HIST])
        zhist = m("zhist", [P, NG, CONV_W - 1])
        edge = m("edge", [P, NG, HIST])
        wr = m("wr", [P, KT, NE])
        cw = m("cw", [P, CONV_W, NG])
        cb = m("cb", [P, NG])
        ps = m("ps", [P, NG])
        stats = m("stats", [P, 2, 6])
        mv = m("mv", [P, 2])
        vareps = m("vareps", [P, 1])
        rstd = m("rstd", [P, 1])

        pw_raw = h1t[:, 0:NG, :]

        r = Place()
        NTE = [P, NT, NE]
        prob = r("prob", NTE)
        sel = r("sel", NTE)
        oh1 = r("oh1", NTE)
        oh2 = r("oh2", NTE)
        mask = r("mask", NTE)
        t_a = r("t_a", NTE)
        t_b = r("t_b", NTE)
        t_c = r("t_c", NTE)
        t_d = r("t_d", NTE)
        gs_a = r("gs_a", [P, NT * NEG])
        gs_b = r("gs_b", [P, NT * NEG])
        gs_c = r("gs_c", [P, NT * NEG])
        gs_d = r("gs_d", [P, NT * NEG])
        row_a = r("row_a", [P, NT])
        row_b = r("row_b", [P, NT])
        row_c = r("row_c", [P, NT])
        row_d = r("row_d", [P, NT])
        slot_f = r("slot_f", [P, 2, NT])
        slot_i = r("slot_i", [P, 2, NT], I32)
        blk_i = r("blk_i", [P, 2, NT], I32)
        rem_i = r("rem_i", [P, 2, NT], I32)
        blk_f = r("blk_f", [P, 2, NT])
        rem_f = r("rem_f", [P, 2, NT])
        gates = r("gates", [P, 2, NT])
        dest = r("dest", [P, 2, NT])
        bias_bc = r("bias_bc", [P, NE])
        upper = r("upper", [P, P])
        ones = r("ones", [P, P])
        iota_p = r("iota_p", [P, P])
        iota_e = r("iota_e", [P, NE])
        iota_b = r("iota_b", [P, NBP])
        cnt = r("cnt", [P, NE])
        nblk = r("nblk", [P, NE])
        end = r("end", [P, NE])
        start = r("start", [P, NE])
        over = r("over", [P, NE, NE])
        tb_a = r("tb_a", [P, NBP, NE])
        tb_b = r("tb_b", [P, NBP, NE])
        f_e = r("f_e", [P, NBP])
        f_first = r("f_first", [P, NBP])
        f_last = r("f_last", [P, NBP])
        f_t = r("f_t", [P, NBP])
        lst = r("lst", [P, 2 * NBP])
        iota_k = r("iota_k", [P, NE])
        hot_r = r("hot_r", [P, 2, P])
        hot_b = r("hot_b", [P, 2, 2, NBP])

        e = Place()
        xg = e("xg", [P, D])
        xt_hi = e("xt_hi", [P, KT, P], F32R)
        xt_lo = e("xt_lo", [P, KT, P], F32R)
        act_a = e("act_a", [P, DE])
        hid = e("hid", [P, DE])
        ht_hi = e("ht_hi", [P, FT, P], F32R)
        ht_lo = e("ht_lo", [P, FT, P], F32R)
        yrow = e("yrow", [P, D])
        g_2 = e("g_2", [P, D])
        b_2 = e("b_2", [P, D])
        f_h = e("f_h", [P, 2, D])
        f_y0 = e("f_y0", [P, D])
        f_y1 = e("f_y1", [P, D])
        fstats = e("fstats", [P, 2, 6])
        fmv = e("fmv", [P, 2])
        fve = e("fve", [P, 1])
        frstd = e("frstd", [P, 1])

        acc = [ctx.enter_context(nc.psum_tensor(f"acc{i}", [P, 512], F32)) for i in range(4)]
        aux = ctx.enter_context(nc.psum_tensor("aux", [P, 512], F32))
        tp = [ctx.enter_context(nc.psum_tensor(f"tp{i}", [P, 4, P], F32)) for i in range(2)]
        logits = ctx.enter_context(nc.psum_tensor("logits", [P, 512], F32))

        ht_v = [a[:, RING1:RING1 + 2, :].rearrange("p u (k t) -> p (u k) t", t=CHUNK) for a in (ring_hi, ring_lo)]
        mix_v = [a[:, RING1 + 2:RING, :].rearrange("p u (k t) -> p (u k) t", t=CHUNK) for a in (ring_hi, ring_lo)]

        s_gin = sem("ln_in_loaded")
        s_const = sem("const_loaded")
        s_cset = sem("const_set")
        s_pw = sem("pool_w_split")
        s_stage = [sem("stage0_in"), sem("stage1_in")]
        s_hi = sem("unit_hi")
        s_lo = sem("unit_lo")
        s_used = sem("unit_used")
        s_x = [sem("x_in0"), sem("x_in1")]
        s_h = sem("h_rows")
        s_h0out = [sem(f"h0_out{t}") for t in range(TPC)]
        s_tr = sem("h_transposed")
        s_trhi = sem("h_t_hi")
        s_trlo = sem("h_t_lo")
        s_sec = [sem(f"sec_{n}") for n in ("c", "u", "v", "b")]
        s_cv = sem("conv_rows")
        s_free = [sem(f"sec_{n}_free") for n in ("c", "u", "v")] + [s_cv]
        s_z = sem("z_ready")
        s_zt = sem("conv_last_tap")
        s_pool = sem("pooled")
        s_pohi = sem("pooled_hi_done")
        s_polo = sem("pooled_lo_done")
        s_pm = sem("pool_mapped")
        s_pmhi = sem("pool_mix_hi")
        s_cvhi = sem("conv_mix_hi")
        s_mix = sem("mix_lo")
        s_out = sem("out_acc")
        s_res = sem("res_taken")
        s_hres = [sem(f"hres_in{t}") for t in range(TPC)]
        s_ve = sem("var_eps")
        s_rstd = sem("rstd_ready")
        s_h1 = sem("h1_rows")
        s_h1out = [sem(f"h1_out{t}") for t in range(TPC)]
        s_h1t = sem("h1_transposed")
        s_h1tc = sem("h1_t_copied")
        s_log = sem("logits_done")
        s_dve = sem("dve_chain")
        s_pool_c = sem("pool_chain")
        s_dve_past = sem("dve_past")
        s_pool_past = sem("pool_past")
        s_rin = sem("route_consts_in")
        s_rset = sem("route_consts_set")
        s_ex = sem("exp_in")
        s_exd = sem("exp_done")
        s_mask = sem("mask_ready")
        s_pre = sem("ranks_done")
        s_hot = sem("one_hots")
        s_lst = sem("list_step")
        s_tab = sem("tables_ready")
        s_zero = sem("xg_zeroed")
        s_gn = sem("gather_index")
        s_gat = sem("gathered")
        s_xt = sem("x_transposed")
        s_xthi = sem("x_t_hi")
        s_xtlo = sem("x_t_lo")
        s_w1 = sem("w1_used")
        s_w3 = sem("w3_used")
        s_w2 = sem("w2_used")
        s_silu = sem("silu_done")
        s_hid = sem("hid_rows")
        s_htr = sem("hid_transposed")
        s_hthi = sem("hid_t_hi")
        s_htlo = sem("hid_t_lo")
        s_y = sem("y_rows")
        s_pn = sem("put_index")
        s_put = sem("y_put")
        s_yfree = sem("y_rows_free")
        s_allput = sem("all_rows_put")
        s_fg = sem("ln2_in")
        s_fh = [sem("final_h0"), sem("final_h1")]
        s_fy0 = sem("final_y0")
        s_fy1 = sem("final_y1")
        s_fu0 = sem("final_y0_used")
        s_fu1 = sem("final_y1_used")
        s_fve = sem("final_var_eps")
        s_fr = sem("final_rstd")
        s_fo = sem("final_rows")
        s_store = [sem("stored0"), sem("stored1")]

        block = ctx.enter_context(nc.Block())

        def bc(ap, n=P):
            return ap.rearrange("(a d) -> a d", a=1).to_broadcast([n, ap.shape[0]])

        N_CONST = 7

        @block.sync
        def _(sp):
            def load_mixer(j):
                if j < 8:
                    s0 = 2 if j % 2 == 0 else 0
                    dst = stage[:, j % 2, :].rearrange("p (k s c) -> p k s c", k=KT, s=2)
                    for i in range(2):
                        sp.dma_start(dst[:, :, i], w_in_v[:, :, s0 + i, j // 2, :]).then_inc(s_stage[j % 2], 16)
                else:
                    n, b = divmod(j - 8, 2)
                    dst = stage[:, j % 2, :].rearrange("p (a r c) -> p a r c", a=2, r=2)
                    for i in range(2):
                        sp.dma_start(dst[:, i], w_out_v[:, b, n, i]).then_inc(s_stage[j % 2], 16)

            for j in range(CU):
                if j >= 2:
                    sp.wait_ge(s_lo, j - 1)
                load_mixer(j)
            with sp.Fori(1, NCH) as c:
                for j in range(CU):
                    sp.wait_ge(s_lo, c * CU + j - 1)
                    load_mixer(j)
            with sp.Fori(0, NE) as ex:
                for j in range(EU):
                    sp.wait_ge(s_lo, ex * EU + MU + j - 1)
                    v = (w1_v, w3_v, w2_v)[j // 2]
                    half_k = v.shape[2] // 2
                    src = v[bass.ds(ex, 1), :, (j % 2) * half_k:(j % 2 + 1) * half_k, :]
                    dst = stage[:, j % 2, :].rearrange("p (k c) -> p k c", k=half_k)
                    sp.dma_start(dst, src.rearrange("e p k c -> p (e k) c")).then_inc(s_stage[j % 2], 16)

            for t in range(TPC):
                sp.wait_ge(s_h1out[t], 16 * NCH)
            sp.dma_start(g_2[:], bc(ln2_g[0])).then_inc(s_fg, 16)
            sp.dma_start(b_2[:], bc(ln2_b[0])).then_inc(s_fg, 16)
            for t in range(NT):
                if t >= 2:
                    sp.wait_ge(s_store[t % 2], 16 * (t // 2))
                sp.dma_start(f_h[:, t % 2, :], h1_dram[t * P:(t + 1) * P, :]).then_inc(s_fh[t % 2], 16)
                if t == 0:
                    sp.wait_ge(s_allput, 1)
                if t >= 1:
                    sp.wait_ge(s_fu0, t)
                sp.dma_start(f_y0[:], y_dram[t * P:(t + 1) * P, :]).then_inc(s_fy0, 16)
                if t >= 1:
                    sp.wait_ge(s_fu1, t)
                sp.dma_start(f_y1[:], y_dram[SEQ + t * P:SEQ + (t + 1) * P, :]).then_inc(s_fy1, 16)
                if t >= 1:
                    sp.wait_ge(s_fo, t)
                    sp.dma_start(out_rows[(t - 1) * P:t * P, :], f_h[:, (t - 1) % 2, :])\
                        .then_inc(s_store[(t - 1) % 2], 16)
            sp.wait_ge(s_fo, NT)
            sp.dma_start(out_rows[(NT - 1) * P:, :], f_h[:, (NT - 1) % 2, :]).then_inc(s_store[(NT - 1) % 2], 16)
            sp.wait_ge(s_store[0], 16 * (NT // 2))
            sp.wait_ge(s_store[1], 16 * (NT // 2))

        @block.tensor
        def _(pe):
            def three(dst, w_hi, w_lo, x_hi, x_lo, start, stop):
                nc.tensor.matmul(dst, w_hi, x_hi, start=start, stop=False)
                nc.tensor.matmul(dst, w_hi, x_lo, start=False, stop=False)
                return nc.tensor.matmul(dst, w_lo, x_hi, start=False, stop=stop)

            def unit_cols(slot, lo, n):
                return [a[:, slot, lo:lo + n] for a in (ring_hi, ring_lo)]

            def section(slot, which, bank):
                for k in range(KT):
                    w = unit_cols(slot, (2 * k + which) * P, P)
                    mm = three(acc[bank][:], *w, ht_v[0][:, k, :], ht_v[1][:, k, :], k == 0, k == KT - 1)
                return mm

            def transpose_tile(rows, sem_out):
                for b in range(2):
                    for q in range(4):
                        k = 4 * b + q
                        mm = nc.tensor.transpose(tp[b][:, q, :], rows[:, k * P:(k + 1) * P], ident[:])
                    mm.then_inc(sem_out, 1)

            def tr_tile(c, t):
                pe.wait_ge(s_h, c * TPC + t + 1)
                if not (isinstance(c, int) and c == 0 and t == 0):
                    pe.wait_ge(s_trlo, (c * TPC + t) * 2)
                if t == 0 and not (isinstance(c, int) and c <= 1):
                    pe.wait_ge(s_h1tc, (c - 1) * TPC * 2)
                transpose_tile(hrow[:, t % 2, :], s_tr)

            def pool_map(c, g):
                pe.wait_ge(s_polo, c * NG + g + 1)
                if not (isinstance(c, int) and c == 0 and g == 0):
                    pe.wait_ge(s_mix, (c * NG + g) * 2)
                three(aux[:], pw_hi[:, g, :], pw_lo[:, g, :], mix_v[0][:, g, :], mix_v[1][:, g, :], True, True)\
                    .then_inc(s_pm, 1)

            def h1_tile(c, t):
                pe.wait_ge(s_h1, c * TPC + t + 1)
                if t >= 1:
                    pe.wait_ge(s_h1tc, (c * TPC + t) * 2)
                transpose_tile(hres[:, t, :], s_h1t)

            def route_tile(c, t):
                pe.wait_ge(s_h1tc, (c * TPC + t + 1) * 2)
                tile = (c * TPC + t)
                dst = logits[:, bass.ds(tile * NE, NE)]
                for k in range(KT):
                    mm = nc.tensor.matmul(dst, h1t[:, k, :], wr[:, k, :], start=(k == 0), stop=(k == KT - 1))
                mm.then_inc(s_log, 1)

            LAST = NCH - 1

            def chunk(c, first, last):
                for j in range(8):
                    g = j // 2
                    pe.wait_ge(s_lo, c * CU + j + 1)
                    if j == 0:
                        pe.wait_ge(s_trlo, (c + 1) * TPC * 2)
                    slot = j % RING1
                    for which in range(2):
                        sct = (j % 2) * 2 + which
                        if g == 0 and not first:
                            pe.wait_ge(s_res, c * 2 * TPC - TPC + sct + 1)
                        if g > 0:
                            pe.wait_ge(s_free[sct], c * NG + g)
                        section(slot, which, sct).then_inc(s_sec[sct], 1)
                    if j % 2 == 0 and g > 0:
                        pool_map(c, g - 1)
                    if not first:
                        if 3 <= j < 7:
                            route_tile(c - 1, j - 3)
                        if 2 <= j < 6:
                            h1_tile(c - 1, j - 2)
                for j in range(8, CU):
                    n, b = divmod(j - 8, 2)
                    if j == 8:
                        if not last:
                            tr_tile(c + 1, 0)
                        pe.wait_ge(s_mix, (c * NG + 3) * 2)
                    if j == 9:
                        pe.wait_ge(s_mix, (c * NG + 4) * 2)
                    pe.wait_ge(s_lo, c * CU + j + 1)
                    for t in range(TPC):
                        if j == 8:
                            pe.wait_ge(s_free[t], (c + 1) * NG)
                        if j == 10:
                            pe.wait_ge(s_res, c * 2 * TPC + t + 1)
                        for a in range(2):
                            for q in range(2):
                                k = 4 * a + 2 * b + q
                                w = [mix_v[i][:, k, t * P:(t + 1) * P] for i in range(2)]
                                xs = unit_cols(j % RING1, (2 * a + q) * 512, 512)
                                mm = three(acc[t][:], *w, *xs, b == 0 and a == 0 and q == 0, b == 1 and a == 1 and q == 1)
                        if b == 1:
                            mm.then_inc(s_out, 1)
                        if j == 8 and t == 1:
                            pool_map(c, 3)
                    if b == 0:
                        mm.then_inc(s_used, 1)
                    if not last and j < CU - 1:
                        tr_tile(c + 1, j - 7)

            pe.wait_ge(s_cset, 1)
            for t in range(TPC):
                tr_tile(0, t)
            pe.wait_ge(s_const, 16 * N_CONST)
            pe.wait_ge(s_pw, 2)
            chunk(0, True, False)
            with pe.Fori(1, NCH - 1) as c:
                chunk(c, False, False)
            chunk(LAST, False, True)
            for t in range(TPC):
                h1_tile(LAST, t)
                route_tile(LAST, t)

            pe.wait_ge(s_rset, 3)
            pe.wait_ge(s_mask, 1)
            flat = mask[:].rearrange("p t e -> p (t e)")
            nc.tensor.matmul(acc[0][:, 0:256], upper[:], flat, start=True, stop=True)
            nc.tensor.matmul(acc[1][:, 0:256], ones[:], flat, start=True, stop=True).then_inc(s_pre, 1)
            with pe.Fori(0, NT) as t:
                for k in range(2):
                    pe.wait_ge(s_hot, t * 2 + k + 1)
                    nc.tensor.matmul(acc[2 + k][:, 0:2 * NBP], hot_r[:, k, :],
                                     hot_b[:, k].rearrange("p v b -> p (v b)"),
                                     start=True, stop=True).then_inc(s_lst, 1)

            def x_tile(b):
                pe.wait_ge(s_gat, b * 16 + 16)
                if not (isinstance(b, int) and b == 0):
                    pe.wait_ge(s_xtlo, b * 2)
                transpose_tile(xg[:], s_xt)

            def up(b, base, e_of, which, used):
                for h in range(2):
                    pe.wait_ge(s_lo, e_of * EU + MU + 2 * which + h + 1)
                    slot = (base + (2 * which + h)) % RING
                    for q in range(4):
                        k = 4 * h + q
                        xs = [a[:, bass.ds(slot, 1), q * 512:(q + 1) * 512].rearrange("p u c -> p (u c)")
                              for a in (ring_hi, ring_lo)]
                        mm = three(acc[which][:], xt_hi[:, k, :], xt_lo[:, k, :], *xs,
                                   k == 0, k == KT - 1)
                mm.then_inc(used, 1)

            def down(base, e_of):
                for h in range(2):
                    pe.wait_ge(s_lo, e_of * EU + MU + 4 + h + 1)
                    slot = (base + (4 + h)) % RING
                    for q in range(2):
                        k = 2 * h + q
                        for n in range(2):
                            o = q * 1024 + n * 512
                            xs = [a[:, bass.ds(slot, 1), o:o + 512].rearrange("p u c -> p (u c)")
                                  for a in (ring_hi, ring_lo)]
                            mm = three(acc[2 + n][:], ht_hi[:, k, :], ht_lo[:, k, :], *xs,
                                       k == 0, k == FT - 1)
                mm.then_inc(s_w2, 1)

            def hid_tile(b):
                pe.wait_ge(s_hid, b + 1)
                if not (isinstance(b, int) and b == 0):
                    pe.wait_ge(s_htlo, b)
                for q in range(FT):
                    mm = nc.tensor.transpose(aux[:, q * P:(q + 1) * P], hid[:, q * P:(q + 1) * P], ident[:])
                mm.then_inc(s_htr, 1)

            pe.wait_ge(s_tab, 1)
            nb = pe.value_load(nblocks[0:1, 0:1], min_val=NE, max_val=NB)
            x_tile(0)
            pe.wait_ge(s_xtlo, 2)
            up(0, 0, 0, 0, s_w1)
            up(0, 0, 0, 1, s_w3)
            x_tile(1)
            hid_tile(0)
            with pe.Fori(1, nb) as b:
                base = pe.value_load(table[0:1, 0, bass.ds(b, 1)], min_val=0, max_val=RING - 2)
                e_of = pe.value_load(table[0:1, 1, bass.ds(b, 1)], min_val=0, max_val=NE - 1)
                pbase = pe.value_load(table[0:1, 0, bass.ds(b - 1, 1)], min_val=0, max_val=RING - 2)
                pe_of = pe.value_load(table[0:1, 1, bass.ds(b - 1, 1)], min_val=0, max_val=NE - 1)
                pe.wait_ge(s_xtlo, b * 2 + 2)
                pe.wait_ge(s_silu, b)
                up(b, base, e_of, 0, s_w1)
                pe.wait_ge(s_hid, b)
                up(b, base, e_of, 1, s_w3)
                x_tile(b + 1)
                pe.wait_ge(s_htlo, b)
                pe.wait_ge(s_y, b)
                down(pbase, pe_of)
                hid_tile(b)
            lbase = pe.value_load(table[0:1, 0, bass.ds(nb - 1, 1)], min_val=0, max_val=RING - 2)
            pe.wait_ge(s_htlo, nb)
            pe.wait_ge(s_y, nb)
            down(lbase, NE - 1)

        @block.scalar
        def _(act):
            def split_hi(slot_in, landed, slot):
                act.wait_ge(s_stage[slot_in], landed)
                if isinstance(slot, int):
                    nc.scalar.copy(ring_hi[:, slot, :], stage[:, slot_in, :]).then_inc(s_hi, 1)
                else:
                    nc.scalar.copy(ring_hi[:, bass.ds(slot, 1), :], stage[:, slot_in:slot_in + 1, :]).then_inc(s_hi, 1)

            def unit_ahead(c, j, last):
                ja = j + RING1 - 1
                if ja >= CU and last:
                    return
                slot_in = ja % 2
                landed = (c * (CU // 2) + (ja // 2) + 1) * 32
                if not (isinstance(c, int) and c == 0 and j == 0):
                    if j == 0:
                        act.wait_ge(s_out, c * 2 * TPC)
                    elif j < 9:
                        q = (j - 1) // 2
                        act.wait_ge(s_sec[3 if (j - 1) % 2 else 1], c * NG + q + 1)
                    elif j == 10:
                        act.wait_ge(s_out, c * 2 * TPC + TPC)
                    else:
                        act.wait_ge(s_used, c * 2 + (1 if j == 9 else 2))
                split_hi(slot_in, landed, ja % RING1)

            def tr_hi(c, t):
                for b in range(2):
                    act.wait_ge(s_tr, (c * TPC + t) * 2 + b + 1)
                    nc.scalar.copy(ht_v[0][:, 4 * b:4 * b + 4, t * P:(t + 1) * P], tp[b][:]).then_inc(s_trhi, 1)

            def pool_mix_hi(c, g):
                act.wait_ge(s_pm, c * NG + g + 1)
                nc.scalar.activation(mix_v[0][:, g, :], aux[:], ACT.Copy, scale=ps[:, g:g + 1]).then_inc(s_pmhi, 1)

            def conv_mix_hi(c, g):
                act.wait_ge(s_cv, c * NG + g + 1)
                nc.scalar.copy(mix_v[0][:, NG + g, :], cacc[:]).then_inc(s_cvhi, 1)

            def h1t_copy(c, t):
                for b in range(2):
                    act.wait_ge(s_h1t, (c * TPC + t) * 2 + b + 1)
                    nc.scalar.copy(h1t[:, 4 * b:4 * b + 4, :], tp[b][:]).then_inc(s_h1tc, 1)

            def chunk(c, first, last):
                for j in range(CU):
                    unit_ahead(c, j, last)
                    g = j // 2
                    if not first and 3 <= j < 7:
                        h1t_copy(c - 1, j - 3)
                    if j < 8 and j % 2 == 0:
                        if g > 0:
                            conv_mix_hi(c, g - 1)
                        if not (first and g == 0):
                            act.wait_ge(s_cv, c * NG + g)
                        act.wait_ge(s_sec[1], c * NG + g + 1)
                        nc.scalar.copy(zext[:, 2:], acc[1][:]).then_inc(s_free[1], 1)
                    if j < 8 and j % 2 == 1:
                        if g > 0:
                            pool_mix_hi(c, g - 1)
                        act.wait_ge(s_z, c * NG + g + 1)
                        if not (first and g == 0):
                            act.wait_ge(s_mix, (c * NG + g) * 2 - 1)
                        nc.scalar.activation(cacc[:], zext[:, 2:], ACT.Identity, scale=cw[:, 2, g:g + 1],
                                             bias=cb[:, g:g + 1]).then_inc(s_zt, 1)
                        act.wait_ge(s_sec[2], c * NG + g + 1)
                        if not (first and g == 0):
                            act.wait_ge(s_pool, c * NG + g)
                        nc.scalar.copy(vext[:, HIST:], acc[2][:]).then_inc(s_free[2], 1)
                        act.wait_ge(s_pool, c * NG + g + 1)
                        nc.scalar.copy(mix_v[0][:, g, :], sum_a[:, HIST:]).then_inc(s_pohi, 1)
                    if j == 8:
                        conv_mix_hi(c, 3)
                        if not last:
                            tr_hi(c + 1, 0)
                    if j == 9:
                        pool_mix_hi(c, 3)
                    if 9 <= j and not last:
                        tr_hi(c + 1, j - 8)

            for j in range(RING1 - 1):
                split_hi(j % 2, (j // 2 + 1) * 32, j)
            act.wait_ge(s_const, 16 * N_CONST)
            nc.scalar.copy(pw_hi[:], pw_raw).then_inc(s_pw, 1)
            for t in range(TPC):
                tr_hi(0, t)
            chunk(0, True, False)
            with act.Fori(1, NCH - 1) as c:
                chunk(c, False, False)
            chunk(NCH - 1, False, True)
            for t in range(TPC):
                h1t_copy(NCH - 1, t)

            act.wait_ge(s_out, NCH * 2 * TPC)
            for j in range(EU):
                split_hi(j % 2, MU // 2 * 32 + (j // 2 + 1) * 16, j)
                if j == 1:
                    act.wait_ge(s_ex, 1)
                    nc.scalar.activation(prob[:], t_a[:], ACT.Exp).then_inc(s_exd, 1)

            act.wait_ge(s_tab, 1)
            nb = act.value_load(nblocks[0:1, 0:1], min_val=NE, max_val=NB)

            def x_hi(b):
                for h in range(2):
                    act.wait_ge(s_xt, b * 2 + h + 1)
                    nc.scalar.copy(xt_hi[:, 4 * h:4 * h + 4, :], tp[h][:]).then_inc(s_xthi, 1)

            def hid_hi(b):
                act.wait_ge(s_htr, b + 1)
                nc.scalar.copy(ht_hi[:], aux[:].rearrange("p (k t) -> p k t", t=P)).then_inc(s_hthi, 1)

            def silu(b):
                act.wait_ge(s_w1, b + 1)
                if not (isinstance(b, int) and b == 0):
                    act.wait_ge(s_hid, b)
                nc.scalar.activation(act_a[:], acc[0][:], ACT.Silu).then_inc(s_silu, 1)

            def y_rows(b):
                act.wait_ge(s_w2, b + 1)
                act.wait_ge(s_yfree, b + 1)
                for n in range(2):
                    ins = nc.scalar.copy(yrow[:, n * 512:(n + 1) * 512], acc[2 + n][:])
                ins.then_inc(s_y, 1)

            def next_units(e_of, base, js):
                for j in js:
                    split_hi(j % 2, e_of * (EU // 2 * 16) + MU // 2 * 32 + (EU // 2 + j // 2 + 1) * 16, (base + (EU + j)) % RING)

            def turn(b, first):
                base = act.value_load(table[0:1, 0, bass.ds(b, 1)], min_val=0, max_val=RING - 2)
                e_of = act.value_load(table[0:1, 1, bass.ds(b, 1)], min_val=0, max_val=NE - 1)
                fb = act.value_load(table[0:1, 2, bass.ds(b, 1)], min_val=0, max_val=NB)
                sp_ = act.value_load(table[0:1, 3, bass.ds(b, 1)], min_val=0, max_val=1)
                if not first:
                    hid_hi(b - 1)
                    with act.If(sp_ > 0):
                        act.wait_ge(s_w2, fb)
                        next_units(e_of, base, (0, 1))
                    act.nop()
                else:
                    with act.If(sp_ > 0):
                        next_units(e_of, base, (0, 1))
                    act.nop()
                silu(b)
                with act.If(sp_ > 0):
                    next_units(e_of, base, (2, 3))
                act.nop()
                act.wait_ge(s_w3, b + 1)
                x_hi(b + 1)
                with act.If(sp_ > 0):
                    next_units(e_of, base, (4, 5))
                act.nop()
                if not first:
                    y_rows(b - 1)

            x_hi(0)
            turn(0, True)
            with act.Fori(1, nb) as b:
                turn(b, False)
            hid_hi(nb - 1)
            y_rows(nb - 1)

        @block.vector
        def _(dve):
            ch = Chain(dve, s_dve)
            V = nc.vector

            def split_lo(slot_in, count, slot):
                dve.wait_ge(s_hi, count)
                if isinstance(slot, int):
                    hi, lo, raw = ring_hi[:, slot, :], ring_lo[:, slot, :], stage[:, slot_in, :]
                else:
                    hi, lo = (a[:, bass.ds(slot, 1), :] for a in (ring_hi, ring_lo))
                    raw = stage[:, slot_in:slot_in + 1, :]
                V.tensor_tensor(lo, raw, hi.bitcast(F32), ALU.subtract).then_inc(s_lo, 1)

            def unit_ahead(c, j, last):
                ja = j + RING1 - 1
                if ja >= CU and last:
                    return
                split_lo(ja % 2, c * CU + ja + 1, ja % RING1)

            def norm_stats(rows):
                V.bn_stats(stats[:, 0, :], rows[:, 0:512])
                ch.link(V.bn_stats(stats[:, 1, :], rows[:, 512:1024]))
                carry(dve, s_dve_past)
                ch.link(V.bn_aggr(mv[:], stats[:].rearrange("p a b -> p (a b)")))
                V.tensor_scalar(vareps[:], mv[:, 1:2], EPS, None, ALU.add).then_inc(s_ve, 1)

            def norm_rows(n, rows, g, b, done):
                ch.link(V.scalar_tensor_tensor(out=rows, in0=rows, scalar=mv[:, 0:1], in1=g, op0=ALU.subtract, op1=ALU.mult))
                dve.wait_ge(s_rstd, n + 1)
                V.scalar_tensor_tensor(out=rows, in0=rows, scalar=rstd[:], in1=b, op0=ALU.mult, op1=ALU.add).then_inc(done, 1)

            def ln_h(c, t, n):
                rows = hrow[:, t % 2, :]
                dve.wait_ge(s_x[t % 2], (c * 2 + t // 2 + 1) * 16)
                norm_stats(rows)
                norm_rows(n, rows, g_in[:], b_in[:], s_h)

            def ln_h1(c, t, n):
                rows = hres[:, t, :]
                dve.wait_ge(s_res, c * 2 * TPC + TPC + t + 1)
                norm_stats(rows)
                norm_rows(n, rows, g_1[:], b_1[:], s_h1)

            def tr_lo(c, t):
                for b in range(2):
                    dve.wait_ge(s_trhi, (c * TPC + t) * 2 + b + 1)
                    cols = (slice(None), slice(4 * b, 4 * b + 4), slice(t * P, (t + 1) * P))
                    V.tensor_tensor(ht_v[1][cols], tp[b][:], ht_v[0][cols].bitcast(F32), ALU.subtract).then_inc(s_trlo, 1)

            def z_rows(c, g):
                dve.wait_ge(s_sec[0], c * NG + g + 1)
                dve.wait_ge(s_free[1], c * NG + g + 1)
                ch.mark(V.tensor_copy(zext[:, 0:2], zhist[:, g, :]))
                V.tensor_tensor(zext[:, 2:], zext[:, 2:], acc[0][:], ALU.mult).then_inc(s_z, 1)
                dve.wait_ge(s_z, c * NG + g + 1)
                V.tensor_copy(zhist[:, g, :], zext[:, CHUNK:]).then_inc(s_free[0], 1)

            def pool_rows(c, g):
                w = WINDOWS[g]
                n = HIST + CHUNK
                dve.wait_ge(s_free[2], c * NG + g + 1)
                if not (isinstance(c, int) and c == 0 and g == 0):
                    dve.wait_ge(s_pohi, c * NG + g)
                ch.link(V.tensor_copy(vext[:, 0:HIST], vhist[:, g, :]))
                src, k = vext, 1
                bufs = [sum_b, sum_a]
                levels = w.bit_length() - 1
                if levels % 2 == 0:
                    bufs = bufs[::-1]
                for i in range(levels):
                    dst = bufs[i % 2]
                    lo = 2 * k - 1
                    ch.link(V.tensor_tensor(dst[:, lo:n], src[:, lo:n], src[:, lo - k:n - k], ALU.add))
                    src, k = dst, 2 * k
                ch.mark(V.scalar_tensor_tensor(out=sum_a[:, 2 * HIST:], in0=src[:, 2 * HIST:], scalar=1.0 / w,
                                               in1=vext[:, 2 * HIST:], op0=ALU.mult, op1=ALU.subtract))
                ch.link(V.tensor_tensor(sum_a[:, HIST:2 * HIST], src[:, HIST:2 * HIST], edge[:, g, :], ALU.mult))
                ch.link(V.tensor_tensor(sum_a[:, HIST:2 * HIST], sum_a[:, HIST:2 * HIST], vext[:, HIST:2 * HIST], ALU.subtract))
                V.tensor_copy(vhist[:, g, :], vext[:, CHUNK:]).then_inc(s_pool, 1)

            def conv_rows(c, g):
                dve.wait_ge(s_zt, c * NG + g + 1)
                ch.link(V.scalar_tensor_tensor(out=cacc[:], in0=zext[:, 1:1 + CHUNK], scalar=cw[:, 1, g:g + 1],
                                               in1=cacc[:], op0=ALU.mult, op1=ALU.add))
                ch.link(V.scalar_tensor_tensor(out=cacc[:], in0=zext[:, 0:CHUNK], scalar=cw[:, 0, g:g + 1],
                                               in1=cacc[:], op0=ALU.mult, op1=ALU.add))

            def pooled_split(c, g):
                dve.wait_ge(s_pohi, c * NG + g + 1)
                V.tensor_tensor(mix_v[1][:, g, :], sum_a[:, HIST:], mix_v[0][:, g, :].bitcast(F32),
                                ALU.subtract).then_inc(s_polo, 1)

            def gate_rows(c, g):
                dve.wait_ge(s_sec[3], c * NG + g + 1)
                V.tensor_tensor(cacc[:], cacc[:], acc[3][:], ALU.mult).then_inc(s_cv, 1)


            def conv_lo(c, g):
                dve.wait_ge(s_cvhi, c * NG + g + 1)
                V.tensor_tensor(mix_v[1][:, NG + g, :], cacc[:], mix_v[0][:, NG + g, :].bitcast(F32),
                                ALU.subtract).then_inc(s_mix, 1)

            def pool_mix_lo(c, g):
                dve.wait_ge(s_pmhi, c * NG + g + 1)
                V.scalar_tensor_tensor(out=mix_v[1][:, g, :], in0=aux[:], scalar=ps[:, g:g + 1],
                                       in1=mix_v[0][:, g, :].bitcast(F32), op0=ALU.mult,
                                       op1=ALU.subtract).then_inc(s_mix, 1)

            def residual(c, n, t):
                if n == 0:
                    dve.wait_ge(s_hres[t], c * 16 + 16)
                dve.wait_ge(s_out, c * 2 * TPC + n * TPC + t + 1)
                cols = hres[:, t, n * 512:(n + 1) * 512]
                V.scalar_tensor_tensor(out=cols, in0=cols, scalar=ALPHA, in1=acc[t][:], op0=ALU.mult,
                                       op1=ALU.add).then_inc(s_res, 1)

            def chunk(c, first, last):
                n = [TPC if first else (c - 1) * 8 + 2 * TPC]

                def nth():
                    n[0] = n[0] + 1
                    return n[0] - 1
                for j in range(CU):
                    unit_ahead(c, j, last)
                    g = j // 2
                    if j < 8 and j % 2 == 0:
                        z_rows(c, g)
                        if g > 0:
                            conv_lo(c, g - 1)
                    if j < 8 and j % 2 == 1:
                        if g > 0:
                            pool_mix_lo(c, g - 1)
                        pool_rows(c, g)
                        conv_rows(c, g)
                        pooled_split(c, g)
                        if g == 3 and first:
                            for gg, w in enumerate(WINDOWS):
                                ins = V.memset(edge[:, gg, :], 1.0 / w)
                            ch.link(ins)
                    if not first and j < 4:
                        ln_h1(c - 1, j, nth())
                    if j < 8 and j % 2 == 1:
                        gate_rows(c, g)
                    if not last:
                        if j in (5, 7):
                            ln_h(c + 1, (j - 5) // 2, nth())
                        if j == 8:
                            conv_lo(c, 3)
                            tr_lo(c + 1, 0)
                        if j == 9:
                            pool_mix_lo(c, 3)
                            ln_h(c + 1, 2, nth())
                            tr_lo(c + 1, 1)
                        if j == 10:
                            for t in range(TPC):
                                residual(c, 0, t)
                            ln_h(c + 1, 3, nth())
                            tr_lo(c + 1, 2)
                        if j == 11:
                            tr_lo(c + 1, 3)
                            for t in range(TPC):
                                residual(c, 1, t)
                    else:
                        if j == 8:
                            conv_lo(c, 3)
                        if j == 9:
                            pool_mix_lo(c, 3)
                        if j in (10, 11):
                            for t in range(TPC):
                                residual(c, j - 10, t)

            dve.wait_ge(s_gin, 32)
            for t in range(2):
                ln_h(0, t, t)
            for j in range(RING1 - 1):
                split_lo(j % 2, j + 1, j)
            dve.wait_ge(s_pw, 1)
            V.tensor_tensor(pw_lo[:], pw_raw, pw_hi[:].bitcast(F32), ALU.subtract).then_inc(s_pw, 1)
            dve.wait_ge(s_cset, 2)
            for g, w in enumerate(WINDOWS):
                ins = V.tensor_scalar(edge[:, g, :], edge[:, g, :], float(w), None, ALU.min)
            ch.link(ins)
            ch.link(V.reciprocal(edge[:], edge[:]))
            tr_lo(0, 0)
            ln_h(0, 2, 2)
            tr_lo(0, 1)
            ln_h(0, 3, 3)
            tr_lo(0, 2)
            tr_lo(0, 3)
            chunk(0, True, False)
            with dve.Fori(1, NCH - 1) as c:
                ch.enter(c - 1, DVE_PER_CHUNK)
                chunk(c, False, False)
                ch.leave(NCH - 2)
            chunk(NCH - 1, False, True)
            for t in range(TPC):
                ln_h1(NCH - 1, t, 8 * NCH - TPC + t)

            dve.wait_ge(s_log, NT)
            for t in range(TPC):
                dve.wait_ge(s_h1out[t], 16 * NCH)
            dve.wait_ge(s_rset, 4)
            dve.wait_ge(s_rin, 16)
            lg = logits[:, 0:NT * NE].rearrange("p (t e) -> p t e", e=NE)

            def over_e(a):
                return a[:].unsqueeze(2).to_broadcast(NTE)

            def tt(out, a, b, op):
                ch.link(V.tensor_tensor(out, a, b, op))

            def red(out, a, op):
                ch.link(V.tensor_reduce(out, a, AX.X, op))

            iota = iota_e[:].unsqueeze(1).to_broadcast(NTE)
            red(row_a[:], lg, ALU.max)
            ins = V.tensor_tensor(t_a[:], lg, over_e(row_a), ALU.subtract)
            ins.then_inc(s_ex, 1)
            dve.wait_ge(s_exd, 1)
            red(row_b[:], prob[:], ALU.add)
            ch.link(V.reciprocal(row_b[:], row_b[:]))
            tt(prob[:], prob[:], over_e(row_b), ALU.mult)
            tt(sel[:], prob[:], bias_bc[:].unsqueeze(1).to_broadcast(NTE), ALU.add)
            s4 = sel[:].rearrange("p t (g i) -> p (t g) i", i=EPG)
            V.tensor_tensor(gs_a[:], s4[:, :, 0], s4[:, :, 1], ALU.max)
            V.tensor_tensor(gs_b[:], s4[:, :, 0], s4[:, :, 1], ALU.min)
            V.tensor_tensor(gs_c[:], s4[:, :, 2], s4[:, :, 3], ALU.max)
            tt(gs_d[:], s4[:, :, 2], s4[:, :, 3], ALU.min)
            tt(gs_b[:], gs_b[:], gs_d[:], ALU.max)
            tt(gs_d[:], gs_a[:], gs_c[:], ALU.min)
            tt(gs_b[:], gs_b[:], gs_d[:], ALU.max)
            tt(gs_a[:], gs_a[:], gs_c[:], ALU.max)
            tt(gs_a[:], gs_a[:], gs_b[:], ALU.add)

            def first_hot(vals, shape, top, eq, hot, iota_ap, far):
                over = lambda a: a[:].unsqueeze(2).to_broadcast(shape)
                red(top[:], vals, ALU.max)
                tt(eq, vals, over(top), ALU.is_equal)
                ch.link(V.scalar_tensor_tensor(out=eq, in0=eq, scalar=-far, in1=iota_ap, op0=ALU.mult, op1=ALU.add))
                red(top[:], eq, ALU.min)
                ch.link(V.tensor_scalar(top[:], top[:], far, None, ALU.add))
                tt(hot, iota_ap, over(top), ALU.is_equal)

            g3 = [P, NT, NEG]
            gv = lambda a: a[:].rearrange("p (t g) -> p t g", g=NEG)
            first_hot(gv(gs_a), g3, row_a, gv(gs_b), gv(gs_c), iota_e[:, 0:NEG].unsqueeze(1).to_broadcast(g3), 64.0)
            ch.link(V.tensor_scalar(gs_c[:], gs_c[:], BIG, -BIG, ALU.mult, ALU.add))
            tt(t_b[:].rearrange("p t (g i) -> p (t g) i", i=EPG), s4,
               gs_c[:].unsqueeze(2).to_broadcast([P, NT * NEG, EPG]), ALU.add)
            first_hot(t_b[:], NTE, row_a, t_c[:], oh1[:], iota, 64.0)
            ch.link(V.scalar_tensor_tensor(out=t_b[:], in0=oh1[:], scalar=-3 * BIG, in1=t_b[:], op0=ALU.mult, op1=ALU.add))
            first_hot(t_b[:], NTE, row_a, t_c[:], oh2[:], iota, 64.0)
            V.tensor_tensor(mask[:], oh1[:], oh2[:], ALU.add).then_inc(s_mask, 1)
            tt(t_c[:], oh1[:], prob[:], ALU.mult)
            tt(t_d[:], oh2[:], prob[:], ALU.mult)
            red(row_a[:], t_c[:], ALU.add)
            red(row_b[:], t_d[:], ALU.add)
            tt(row_c[:], row_a[:], row_b[:], ALU.add)
            ch.link(V.reciprocal(row_c[:], row_c[:]))
            tt(gates[:, 0, :], row_a[:], row_c[:], ALU.mult)
            tt(gates[:, 1, :], row_b[:], row_c[:], ALU.mult)
            dve.wait_ge(s_pre, 1)
            ch.link(V.tensor_copy(t_a[:], acc[0][:, 0:256].rearrange("p (t e) -> p t e", e=NE)))
            ch.link(V.tensor_copy(t_b[:], acc[1][:, 0:256].rearrange("p (t e) -> p t e", e=NE)))
            ch.link(V.tensor_copy(t_c[:], t_b[:]))
            src, dst = t_c, t_d
            for k in (1, 2, 4, 8):
                V.tensor_copy(dst[:, 0:k, :], src[:, 0:k, :])
                tt(dst[:, k:, :], src[:, k:, :], src[:, :NT - k, :], ALU.add)
                src, dst = dst, src
            ch.link(V.tensor_copy(cnt[:], src[:, NT - 1, :]))
            tt(t_b[:], src[:], t_b[:], ALU.subtract)
            tt(t_a[:], t_a[:], t_b[:], ALU.add)
            tt(over[:], cnt[:].unsqueeze(2).to_broadcast([P, NE, NE]),
               iota_k[:].unsqueeze(1).to_broadcast([P, NE, NE]), ALU.is_gt)
            red(nblk[:], over[:], ALU.add)
            ch.link(V.tensor_scalar(nblk[:], nblk[:], 1.0, None, ALU.max))
            ch.link(V.tensor_tensor_scan(end[:], ones[:, 0:NE], nblk[:], 0.0, ALU.mult, ALU.add))
            tt(start[:], end[:], nblk[:], ALU.subtract)
            ch.link(V.tensor_scalar(cnt[:], start[:], float(P), None, ALU.mult))
            tt(t_a[:], t_a[:], cnt[:].unsqueeze(1).to_broadcast(NTE), ALU.add)
            tt(t_b[:], t_a[:], oh1[:], ALU.mult)
            tt(t_c[:], t_a[:], oh2[:], ALU.mult)
            red(slot_f[:, 0, :], t_b[:], ALU.add)
            red(slot_f[:, 1, :], t_c[:], ALU.add)
            ch.link(V.tensor_copy(slot_i[:], slot_f[:]))
            ch.link(V.tensor_scalar(blk_i[:], slot_i[:], 7, None, ALU.logical_shift_right))
            ch.link(V.tensor_scalar(rem_i[:], slot_i[:], P - 1, None, ALU.bitwise_and))
            ch.link(V.tensor_copy(blk_f[:], blk_i[:]))
            ch.link(V.tensor_copy(rem_f[:], rem_i[:]))
            ch.link(V.memset(lst[:], 0.0))
            ROUTE = 6
            with dve.Fori(0, NT) as t:
                ch.enter(t, ROUTE)
                for k in range(2):
                    blk = blk_f[:, k, bass.ds(t, 1)]
                    ch.link(V.tensor_scalar(hot_r[:, k, :], iota_p[:], rem_f[:, k, bass.ds(t, 1)], None, ALU.is_equal))
                    ch.link(V.tensor_scalar(hot_b[:, k, 0, :], iota_b[:], blk, dest[:, k, bass.ds(t, 1)], ALU.is_equal, ALU.mult))
                    V.tensor_scalar(hot_b[:, k, 1, :], iota_b[:], blk, gates[:, k, bass.ds(t, 1)],
                                    ALU.is_equal, ALU.mult).then_inc(s_hot, 1)
                for k in range(2):
                    dve.wait_ge(s_lst, t * 2 + k + 1)
                    ch.link(V.tensor_tensor(lst[:], lst[:], acc[2 + k][:, 0:2 * NBP], ALU.add))
                ch.leave(NT)
            v = lst[:, 0:NBP]
            ch.link(V.tensor_scalar(f_t[:], v, 0.5, OOB, ALU.is_lt, ALU.mult))
            ch.link(V.scalar_tensor_tensor(out=f_t[:], in0=v, scalar=-1.0, in1=f_t[:], op0=ALU.add, op1=ALU.add))
            ch.link(V.tensor_copy(put_idx[:], f_t[:]))
            ch.link(V.tensor_scalar(f_e[:], v, SEQ + 0.5, -float(SEQ), ALU.is_gt, ALU.mult))
            tt(f_e[:], f_e[:], f_t[:], ALU.add)
            ch.link(V.tensor_copy(gat_idx[:], f_e[:]))
            ch.link(V.tensor_copy(gate[:], lst[:, NBP:]))
            B3 = [P, NBP, NE]
            ends = end[:].unsqueeze(1).to_broadcast(B3)
            blocks = iota_b[:].unsqueeze(2).to_broadcast(B3)
            tt(tb_a[:], ends, blocks, ALU.is_le)
            red(f_e[:], tb_a[:], ALU.add)
            tt(tb_b[:], tb_a[:], nblk[:].unsqueeze(1).to_broadcast(B3), ALU.mult)
            red(f_first[:], tb_b[:], ALU.add)
            ch.link(V.tensor_scalar(f_t[:], iota_b[:], 1.0, None, ALU.add))
            tt(tb_a[:], ends, f_t[:].unsqueeze(2).to_broadcast(B3), ALU.is_equal)
            red(f_last[:], tb_a[:, :, 0:NE - 1], ALU.add)
            ch.link(V.tensor_scalar(f_e[:], f_e[:], float(NE - 1), None, ALU.min))
            ch.link(V.tensor_copy(table[:, 1, :], f_e[:]))
            ch.link(V.tensor_scalar(f_first[:], f_first[:], 1.0, None, ALU.max))
            ch.link(V.tensor_copy(table[:, 2, :], f_first[:]))
            ch.link(V.tensor_copy(table[:, 3, :], f_last[:]))
            ch.link(V.tensor_scalar(f_t[:], f_e[:], float(EU), None, ALU.mult))
            ch.link(V.tensor_copy(table[:, 0, :], f_t[:]))
            ch.link(V.tensor_scalar(table[:, 0, :], table[:, 0, :], RING - 1, None, ALU.bitwise_and))
            V.tensor_copy(nblocks[:], end[:, NE - 1:NE]).then_inc(s_tab, 1)

            for j in range(EU):
                split_lo(j % 2, MU + j + 1, j)
            dve.wait_ge(s_tab, 1)
            nb = dve.value_load(nblocks[0:1, 0:1], min_val=NE, max_val=NB)

            def x_lo(b):
                for h in range(2):
                    dve.wait_ge(s_xthi, b * 2 + h + 1)
                    V.tensor_tensor(xt_lo[:, 4 * h:4 * h + 4, :], tp[h][:], xt_hi[:, 4 * h:4 * h + 4, :].bitcast(F32),
                                    ALU.subtract).then_inc(s_xtlo, 1)

            def hid_rows(b):
                dve.wait_ge(s_silu, b + 1)
                dve.wait_ge(s_w3, b + 1)
                if not (isinstance(b, int) and b == 0):
                    dve.wait_ge(s_htr, b)
                col = gate[:, bass.ds(b, 1)]
                V.scalar_tensor_tensor(out=hid[:], in0=act_a[:], scalar=col, in1=acc[1][:], op0=ALU.mult,
                                       op1=ALU.mult).then_inc(s_hid, 1)

            def hid_lo(b):
                dve.wait_ge(s_hthi, b + 1)
                V.tensor_tensor(ht_lo[:], aux[:].rearrange("p (k t) -> p k t", t=P), ht_hi[:].bitcast(F32),
                                ALU.subtract).then_inc(s_htlo, 1)

            def next_units(e_of, base, js):
                for j in js:
                    split_lo(j % 2, e_of * EU + MU + EU + j + 1, (base + (EU + j)) % RING)

            def turn(b, first):
                base = dve.value_load(table[0:1, 0, bass.ds(b, 1)], min_val=0, max_val=RING - 2)
                e_of = dve.value_load(table[0:1, 1, bass.ds(b, 1)], min_val=0, max_val=NE - 1)
                sp_ = dve.value_load(table[0:1, 3, bass.ds(b, 1)], min_val=0, max_val=1)
                if not first:
                    hid_lo(b - 1)
                with dve.If(sp_ > 0):
                    next_units(e_of, base, (0, 1, 2, 3))
                dve.nop()
                hid_rows(b)
                x_lo(b + 1)
                with dve.If(sp_ > 0):
                    next_units(e_of, base, (4, 5))
                dve.nop()

            x_lo(0)
            turn(0, True)
            with dve.Fori(1, nb) as b:
                turn(b, False)
            hid_lo(nb - 1)

            dve.wait_ge(s_fg, 32)
            for t in range(NT):
                rows = f_h[:, t % 2, :]
                dve.wait_ge(s_fh[t % 2], 16 * (t // 2 + 1))
                dve.wait_ge(s_fy0, 16 * (t + 1))
                V.scalar_tensor_tensor(out=rows, in0=rows, scalar=ALPHA, in1=f_y0[:], op0=ALU.mult,
                                       op1=ALU.add).then_inc(s_fu0, 1)
                dve.wait_ge(s_fy1, 16 * (t + 1))
                dve.wait_ge(s_fu0, t + 1)
                V.tensor_tensor(rows, rows, f_y1[:], ALU.add).then_inc(s_fu1, 1)
                dve.wait_ge(s_fu1, t + 1)
                V.bn_stats(fstats[:, 0, :], rows[:, 0:512])
                ch.link(V.bn_stats(fstats[:, 1, :], rows[:, 512:1024]))
                ch.link(V.bn_aggr(fmv[:], fstats[:].rearrange("p a b -> p (a b)")))
                V.tensor_scalar(fve[:], fmv[:, 1:2], EPS, None, ALU.add).then_inc(s_fve, 1)
                ch.link(V.scalar_tensor_tensor(out=rows, in0=rows, scalar=fmv[:, 0:1], in1=g_2[:], op0=ALU.subtract, op1=ALU.mult))
                dve.wait_ge(s_fr, t + 1)
                V.scalar_tensor_tensor(out=rows, in0=rows, scalar=frstd[:], in1=b_2[:], op0=ALU.mult, op1=ALU.add).then_inc(s_fo, 1)

        @block.gpsimd
        def _(pool):
            G = nc.gpsimd
            ch = Chain(pool, s_pool_c)
            for t in range(2):
                pool.dma_start(hrow[:, t, :], x_rows[t * P:(t + 1) * P, :]).then_inc(s_x[t], 16)
            pool.dma_start(g_in[:], bc(ln_in_g)).then_inc(s_gin, 16)
            pool.dma_start(b_in[:], bc(ln_in_b)).then_inc(s_gin, 16)
            ch.link(G.memset(ident[:], 0.0))
            G.affine_select(out=ident[:], in_=ident[:], compare_op=ALU.not_equal, fill=1.0, base=0,
                            pattern=[[-1, P]], channel_multiplier=1).then_inc(s_cset, 1)
            ch.link(G.memset(half[:], -0.5))
            G.memset(vhist[:], 0.0)
            G.memset(zhist[:], 0.0)
            G.iota(edge[:], pattern=[[0, NG], [1, HIST]], base=1, channel_multiplier=0,
                   allow_small_or_imprecise_dtypes=True).then_inc(s_cset, 1)
            with nc.allow_non_contiguous_dma(reason="small vectors by channel"):
                pool.dma_start(cw[:], conv_w[0].rearrange("w (g p) -> p w g", p=P)).then_inc(s_const, 16)
                pool.dma_start(cb[:], conv_b[0].rearrange("(g p) -> p g", p=P)).then_inc(s_const, 16)
                pool.dma_start(ps[:], pool_scale[0].rearrange("(g p) -> p g", p=P)).then_inc(s_const, 16)
            pool.dma_start(pw_raw, pool_w[0].rearrange("g c d -> c g d")).then_inc(s_const, 16)
            pool.dma_start(wr[:], w_router.rearrange("(k p) e -> p k e", p=P)).then_inc(s_const, 16)
            pool.dma_start(g_1[:], bc(ln1_g[0])).then_inc(s_const, 16)
            pool.dma_start(b_1[:], bc(ln1_b[0])).then_inc(s_const, 16)

            def inv_root(n):
                pool.wait_ge(s_ve, n + 1)
                G.tensor_tensor(rstd[:], vareps[:], half[:], ALU.pow).then_inc(s_rstd, 1)

            def tile_rows(c, t):
                return bass.ds((c * TPC + t) * P, P)

            def h_norm(c, t, n):
                inv_root(n)
                pool.wait_ge(s_h, c * TPC + t + 1)
                carry(pool, s_pool_past)
                pool.dma_start(h0_dram[tile_rows(c, t), :], hrow[:, t % 2, :]).then_inc(s_h0out[t], 16)

            def x_load(c, t):
                pool.wait_ge(s_tr, (c * TPC + t - 1) * 2)
                if t >= 2:
                    pool.wait_ge(s_h0out[t - 2], c * 16 + 16)
                else:
                    pool.wait_ge(s_h0out[t + 2], c * 16)
                carry(pool, s_pool_past)
                pool.dma_start(hrow[:, t % 2, :], x_rows[tile_rows(c, t), :]).then_inc(s_x[t % 2], 16)

            def res_load(c, t, first):
                if not first:
                    pool.wait_ge(s_h1out[t], c * 16)
                    pool.wait_ge(s_h1t, ((c - 1) * TPC + t + 1) * 2)
                pool.wait_ge(s_h0out[t], c * 16 + 16)
                carry(pool, s_pool_past)
                pool.dma_start(hres[:, t, :], h0_dram[tile_rows(c, t), :]).then_inc(s_hres[t], 16)

            def h1_norm(c, t, n):
                inv_root(n)
                pool.wait_ge(s_h1, c * TPC + t + 1)
                carry(pool, s_pool_past)
                pool.dma_start(h1_dram[tile_rows(c, t), :], hres[:, t, :]).then_inc(s_h1out[t], 16)

            def chunk(c, first, last):
                n = TPC if first else (c - 1) * 8 + 2 * TPC
                if not last:
                    x_load(c + 1, 0)
                    x_load(c + 1, 1)
                if first:
                    for t in range(TPC):
                        res_load(c, t, True)
                if not first:
                    for t in range(TPC):
                        h1_norm(c - 1, t, n)
                        n = n + 1
                        if t >= 2:
                            res_load(c, t - 2, False)
                if not last:
                    h_norm(c + 1, 0, n)
                    if not first:
                        res_load(c, 2, False)
                    h_norm(c + 1, 1, n + 1)
                    if not first:
                        res_load(c, 3, False)
                    x_load(c + 1, 2)
                    x_load(c + 1, 3)
                    h_norm(c + 1, 2, n + 2)
                    h_norm(c + 1, 3, n + 3)
                else:
                    res_load(c, 2, False)
                    res_load(c, 3, False)

            for t in range(2):
                h_norm(0, t, t)
            x_load(0, 2)
            x_load(0, 3)
            h_norm(0, 2, 2)
            h_norm(0, 3, 3)
            chunk(0, True, False)
            with pool.Fori(1, NCH - 1) as c:
                chunk(c, False, False)
            chunk(NCH - 1, False, True)
            for t in range(TPC):
                h1_norm(NCH - 1, t, 8 * NCH - TPC + t)

            for t in range(TPC):
                pool.wait_ge(s_h1out[t], 16 * NCH)
            pool.wait_ge(s_log, NT)
            pool.dma_start(bias_bc[:], bc(router_bias)).then_inc(s_rin, 16)
            G.iota(iota_e[:], pattern=[[1, NE]], base=0, channel_multiplier=0, allow_small_or_imprecise_dtypes=True)
            G.iota(iota_k[:], pattern=[[P, NE]], base=0, channel_multiplier=0, allow_small_or_imprecise_dtypes=True)
            a = ch.mark(G.memset(upper[:], 1.0))
            G.memset(ones[:], 1.0).then_inc(s_rset, 1)
            ch.need(a)
            G.affine_select(out=upper[:], in_=upper[:], compare_op=ALU.is_gt, fill=0.0, base=0,
                            pattern=[[1, P]], channel_multiplier=-1).then_inc(s_rset, 1)
            G.iota(iota_p[:], pattern=[[1, P]], base=0, channel_multiplier=0, allow_small_or_imprecise_dtypes=True)
            G.iota(iota_b[:], pattern=[[1, NBP]], base=0, channel_multiplier=0,
                   allow_small_or_imprecise_dtypes=True).then_inc(s_rset, 1)
            G.iota(dest[:], pattern=[[SEQ, 2], [P, NT]], base=1, channel_multiplier=1,
                   allow_small_or_imprecise_dtypes=True).then_inc(s_rset, 1)

            pool.wait_ge(s_tab, 1)
            G.memset(xg[:], 0.0).then_inc(s_zero, 1)
            nb = pool.value_load(nblocks[0:1, 0:1], min_val=NE, max_val=NB)

            def gather(b):
                G.tensor_copy(gat_now[:], gat_idx[:, bass.ds(b, 1)]).then_inc(s_gn, 1)
                pool.wait_ge(s_gn, b + 1)
                carry(pool, s_pool_past)
                G.indirect_dma_start(xg[:], None, h1_dram, bass.IndirectOffsetOnAxis(ap=gat_now[:, 0:1], axis=0),
                                     bounds_check=SEQ - 1, oob_is_err=False).then_inc(s_gat, 16)

            def put(b):
                pool.wait_ge(s_y, b + 2)
                G.tensor_copy(put_now[:], put_idx[:, bass.ds(b, 1)]).then_inc(s_pn, 1)
                pool.wait_ge(s_pn, b + 1)
                carry(pool, s_pool_past)
                G.indirect_dma_start(y_dram, bass.IndirectOffsetOnAxis(ap=put_now[:, 0:1], axis=0), yrow[:], None,
                                     bounds_check=2 * SEQ - 1, oob_is_err=False).then_inc(s_put, 16)
                pool.wait_ge(s_put, b * 16 + 16)
                pool.sem_inc(s_yfree, 1)

            pool.sem_inc(s_yfree, 1)
            pool.sem_inc(s_y, 1)
            pool.wait_ge(s_zero, 1)
            gather(0)
            pool.wait_ge(s_gat, 16)
            pool.wait_ge(s_xt, 2)
            gather(1)
            with pool.Fori(1, nb) as b:
                pool.wait_ge(s_xt, b * 2 + 2)
                pool.wait_ge(s_gat, b * 16 + 16)
                gather(b + 1)
                put(b - 1)
            put(nb - 1)
            pool.wait_ge(s_gat, nb * 16 + 16)
            pool.sem_inc(s_allput, 1)
            for t in range(NT):
                pool.wait_ge(s_fve, t + 1)
                G.tensor_tensor(frstd[:], fve[:], half[:], ALU.pow).then_inc(s_fr, 1)


_INS = ["x", "ln_in_g", "ln_in_b", "w_in", "pool_w", "pool_scale", "conv_w", "conv_b", "w_out", "ln1_g", "ln1_b",
        "w_router", "router_bias", "exp_w1", "exp_w3", "exp_w2", "ln2_g", "ln2_b"]


def kernel(**inputs):
    from concourse import bacc
    from concourse.bass_utils import run_bass_kernel_spmd

    nc = bacc.Bacc("TRN2", target_bir_lowering=False, num_devices=1)
    arrays, args = {}, []
    for name in _INS:
        a = np.ascontiguousarray(inputs[name])
        arrays[f"in_{name}"] = a
        args.append(nc.dram_tensor(f"in_{name}", a.shape, mybir.dt.from_np(a.dtype), kind="ExternalInput").ap())
    out = nc.dram_tensor("out", (1, SEQ, D), F32, kind="ExternalOutput").ap()
    build(nc, *args, out)
    r = run_bass_kernel_spmd(nc, [arrays], core_ids=[0])
    return r.results[0]["out"]
```

```python
from contextlib import ExitStack

import numpy as np

import concourse.bass as bass
import concourse.mybir as mybir

F32 = mybir.dt.float32
F32R = mybir.dt.float32r
I32 = mybir.dt.int32
U32 = mybir.dt.uint32
ACT = mybir.ActivationFunctionType
ALU = mybir.AluOpType
AX = mybir.AxisListType

P = 128
SEQ = 2048
D = 1024
KT = D // P
CHUNK = 512
NCH = SEQ // CHUNK
TPC = CHUNK // P
NT = SEQ // P
WINDOWS = (2, 4, 8, 16)
NG = len(WINDOWS)
HIST = 16
CONV_W = 3
NE = 16
NEG = 4
EPG = NE // NEG
DE = 512
FT = DE // P
ALPHA = float(2.0 ** 0.25)
EPS = 1e-5
UNIT = 2048
RING = 8
RING1 = 4
CU = 12
EU = 6
MU = NCH * CU
NB = 48
NBP = NB + 1
HOT_T = NT // 2
OOB = 65536.0
BIG = 1.0e30
DVE_PER_CHUNK = 62


class Chain:

    def __init__(self, eng, sem):
        self.eng, self.sem, self.n, self.turn, self.per = eng, sem, 0, None, 0

    def mark(self, ins):
        ins.then_inc(self.sem, 1)
        self.n += 1
        return self.n if self.turn is None else self.turn * self.per + self.n

    def need(self, value):
        self.eng.wait_ge(self.sem, value)

    def link(self, ins):
        self.need(self.mark(ins))

    def enter(self, turn, per):
        self.turn, self.per, self.at = turn, per, self.n

    def leave(self, turns):
        assert self.n - self.at == self.per, (self.n - self.at, self.per)
        self.turn, self.n = None, self.at + turns * self.per


def carry(eng, sem):
    eng.sem_inc(sem, 1)


def build(nc, x, ln_in_g, ln_in_b, w_in, pool_w, pool_scale, conv_w, conv_b, w_out, ln1_g, ln1_b,
          w_router, router_bias, exp_w1, exp_w3, exp_w2, ln2_g, ln2_b, out):
    h0_dram = nc.dram_tensor("h0_scratch", (SEQ, D), F32).ap()
    h1_dram = nc.dram_tensor("h1_scratch", (SEQ, D), F32).ap()
    sum_dram = nc.dram_tensor("sum_scratch", (SEQ, D), F32).ap()

    x_rows, out_rows = x[0], out[0]
    w_in_v = w_in[0].rearrange("(k p) (s g c) -> p k s g c", p=P, s=4, g=NG)
    w_out_v = w_out[0].rearrange("(a b r p) (n c) -> p b n a r c", p=P, a=2, b=2, n=2)
    w1_v = exp_w1[0].rearrange("e (k p) f -> e p k f", p=P)
    w3_v = exp_w3[0].rearrange("e (k p) f -> e p k f", p=P)
    w2_v = exp_w2[0].rearrange("e (k p) n -> e p k n", p=P)

    with ExitStack() as ctx:
        def sb(name, shape, dt=F32):
            return ctx.enter_context(nc.sbuf_tensor(name, shape, dt))

        def sem(name):
            return ctx.enter_context(nc.semaphore(name))

        ring_hi = sb("ring_hi", [P, RING, UNIT], F32R)
        ring_hi_end = nc.sbuf_base
        ring_lo = sb("ring_lo", [P, RING, UNIT], F32R)
        ring_lo_end = nc.sbuf_base
        stage = sb("stage", [P, 2, UNIT])
        ident = sb("ident", [P, P])
        gate = sb("gate", [P, NBP])
        token = sb("token", [P, NBP], U32)
        gat_now = sb("gat_now", [P, 1], U32)
        put_now = sb("put_now", [P, 1], U32)
        table = sb("table", [P, 4, NBP], I32)
        nblocks = sb("nblocks", [P, 3], I32)
        half = sb("half", [P, 1])
        ARENA = 15488
        arena = sb("arena", [P, ARENA])
        arena_at = nc.sbuf_base - 4 * ARENA

        LOW = ARENA - (EU - 2) * UNIT

        class Place:

            def __init__(self, at=arena_at, end=arena_at + 4 * LOW):
                self.at, self.end = at, end

            def __call__(self, name, shape, dt=F32):
                self.at = (self.at + 31) // 32 * 32
                t = nc.alloc_sbuf_tensor_at(name, shape, dt, offset=self.at)
                self.at += 4 * int(np.prod(shape[1:]))
                assert self.at <= self.end, (name, self.at - self.end)
                return t

        m = Place(end=arena_at + 4 * ARENA)
        g_1 = m("g_1", [P, D])
        b_1 = m("b_1", [P, D])
        hres = m("hres", [P, TPC, D])
        h1t = m("h1t", [P, KT, P])
        wr = m("wr", [P, KT, NE])
        stats = m("stats", [P, 2, 6])
        mv = m("mv", [P, 2])
        vareps = m("vareps", [P, 1])
        rstd = m("rstd", [P, 1])
        assert m.at <= arena_at + 4 * (LOW + UNIT)
        g_in = m("g_in", [P, D])
        b_in = m("b_in", [P, D])
        hrow = m("hrow", [P, 2, D])
        vext = m("vext", [P, HIST + CHUNK])
        sum_a = m("sum_a", [P, HIST + CHUNK])
        sum_b = m("sum_b", [P, HIST + CHUNK])
        zext = m("zext", [P, CONV_W - 1 + CHUNK])
        cacc = m("cacc", [P, CHUNK])
        pw_hi = m("pw_hi", [P, NG, P], F32R)
        pw_lo = m("pw_lo", [P, NG, P], F32R)
        vhist = m("vhist", [P, NG, HIST])
        zhist = m("zhist", [P, NG, CONV_W - 1])
        edge = m("edge", [P, NG, HIST])
        cw = m("cw", [P, CONV_W, NG])
        cb = m("cb", [P, NG])
        ps = m("ps", [P, NG])

        pw_raw = h1t[:, 0:NG, :]

        r = Place(ring_hi_end - 4 * 2 * UNIT, ring_hi_end)
        NTE = [P, NT, NE]
        prob = r("prob", NTE)
        sel = r("sel", NTE)
        oh1 = r("oh1", NTE)
        oh2 = r("oh2", NTE)
        mask = r("mask", NTE)
        t_a = r("t_a", NTE)
        t_b = r("t_b", NTE)
        t_c = r("t_c", NTE)
        t_d = r("t_d", NTE)
        sums = r("sums", [P, NE, NT])
        by_e = r("by_e", [P, NE, NT])
        carries = r("carries", [P, NE, NT])
        gs_a = r("gs_a", [P, NT * NEG])
        gs_b = r("gs_b", [P, NT * NEG])
        gs_c = r("gs_c", [P, NT * NEG])
        gs_d = r("gs_d", [P, NT * NEG])
        row_a = r("row_a", [P, NT])
        row_b = r("row_b", [P, NT])
        row_c = r("row_c", [P, NT])
        row_d = r("row_d", [P, NT])
        slot_f = r("slot_f", [P, 2, NT])
        slot_i = r("slot_i", [P, 2, NT], I32)
        blk_i = r("blk_i", [P, 2, NT], I32)
        rem_i = r("rem_i", [P, 2, NT], I32)
        blk_f = r("blk_f", [P, 2, NT])
        rem_f = r("rem_f", [P, 2, NT])
        gates = r("gates", [P, 2, NT])
        dest = r("dest", [P, 2, NT])
        bias_bc = r("bias_bc", [P, NE])
        r = Place(ring_lo_end - 4 * 2 * UNIT, ring_lo_end)
        h1t_b = r("h1t_b", [P, KT, P])
        upper = r("upper", [P, P])
        ones = r("ones", [P, P])
        iota_p = r("iota_p", [P, P])
        iota_e = r("iota_e", [P, NE])
        iota_b = r("iota_b", [P, NBP + 1])
        cnt = r("cnt", [P, NE])
        nblk = r("nblk", [P, NE])
        end = r("end", [P, NE])
        start = r("start", [P, NE])
        over = r("over", [P, NE, NE])
        tb_a = r("tb_a", [P, NBP + 1, NE])
        eq_b = tb_a[:, 0:NBP].rearrange("p b e -> p (b e)").rearrange("p (t b) -> p t b", b=NBP)
        f_e = r("f_e", [P, NBP + 1])
        f_first = r("f_first", [P, NBP])
        f_next = r("f_next", [P, NBP])
        f_t = r("f_t", [P, NBP])
        iota_k = r("iota_k", [P, NE])
        r = Place()
        hot_r = r("hot_r", [P, 2, NT, P])
        hot_b = r("hot_b", [P, 2, NT, 2, NBP])

        e = Place()
        xg = e("xg", [P, D])
        xt_hi = e("xt_hi", [P, KT, P], F32R)
        xt_lo = e("xt_lo", [P, KT, P], F32R)
        act_a = e("act_a", [P, DE])
        hid = e("hid", [P, DE])
        ht_hi = e("ht_hi", [P, FT, P], F32R)
        ht_lo = e("ht_lo", [P, FT, P], F32R)
        yrow = e("yrow", [P, D])
        fstats = e("fstats", [P, 2, 6])
        fmv = e("fmv", [P, NT, 2])
        fve = e("fve", [P, NT])
        frstd = e("frstd", [P, NT])
        stage_x = Place(arena_at + 4 * LOW, arena_at + 4 * ARENA)("stage_x", [P, EU - 2, UNIT])

        def staged(j):
            return stage[:, j:j + 1, :] if j < 2 else stage_x[:, (j - 1) % 4:(j - 1) % 4 + 1, :]

        e = Place(arena_at + 4 * LOW, arena_at + 4 * ARENA)
        g_2 = e("g_2", [P, D])
        b_2 = e("b_2", [P, D])
        f_rows = Place(ring_hi_end - 4 * RING * UNIT, ring_hi_end)("f_rows", [P, NT, D])

        acc = [ctx.enter_context(nc.psum_tensor(f"acc{i}", [P, 512], F32)) for i in range(4)]
        aux = ctx.enter_context(nc.psum_tensor("aux", [P, 512], F32))
        tp = [ctx.enter_context(nc.psum_tensor(f"tp{i}", [P, 4, P], F32)) for i in range(2)]
        logits = ctx.enter_context(nc.psum_tensor("logits", [P, 512], F32))

        last_banks = [tp, [a[:].rearrange("p (q t) -> p q t", t=P) for a in acc[0:2]]]

        ht_v = [a[:, RING1:RING1 + 2, :].rearrange("p u (k t) -> p (u k) t", t=CHUNK) for a in (ring_hi, ring_lo)]
        mix_v = [a[:, RING1 + 2:RING, :].rearrange("p u (k t) -> p (u k) t", t=CHUNK) for a in (ring_hi, ring_lo)]

        s_gin = sem("ln_in_loaded")
        s_const = sem("const_loaded")
        s_cset = sem("const_set")
        s_pw = sem("pool_w_split")
        s_stage = [sem(f"stage{j}_in") for j in range(EU)]
        s_hi = sem("unit_hi")
        s_lo = sem("unit_lo")
        s_used = sem("unit_used")
        s_x0 = [sem(f"x_first{t}") for t in range(TPC)]
        s_x = [sem("x_in0"), sem("x_in1")]
        s_h = sem("h_rows")
        s_h0out = [sem(f"h0_out{t}") for t in range(TPC)]
        s_tr = sem("h_transposed")
        s_trhi = sem("h_t_hi")
        s_trlo = sem("h_t_lo")
        s_sec = [sem(f"sec_{n}") for n in ("c", "u", "v", "b")]
        s_cv = sem("conv_rows")
        s_free = [sem(f"sec_{n}_free") for n in ("c", "u", "v")] + [s_cv]
        s_z = sem("z_ready")
        s_zt = sem("conv_last_tap")
        s_pool = sem("pooled")
        s_pohi = sem("pooled_hi_done")
        s_polo = sem("pooled_lo_done")
        s_pm = sem("pool_mapped")
        s_pmhi = sem("pool_mix_hi")
        s_cvhi = sem("conv_mix_hi")
        s_mix = sem("mix_lo")
        s_out = sem("out_acc")
        s_res = sem("res_taken")
        s_hres = [sem(f"hres_in{t}") for t in range(TPC)]
        s_ve = sem("var_eps")
        s_rstd = sem("rstd_ready")
        s_h1 = sem("h1_rows")
        s_h1out = [sem(f"h1_out{t}") for t in range(TPC)]
        s_ah = sem("alpha_h1")
        s_ahout = [sem(f"alpha_h1_out{t}") for t in range(TPC)]
        s_h1t = sem("h1_transposed")
        s_h1tc = sem("h1_t_copied")
        s_log = sem("logits_done")
        s_dve = sem("dve_chain")
        s_pool_c = sem("pool_chain")
        s_dve_past = sem("dve_past")
        s_pool_past = sem("pool_past")
        s_rin = sem("route_consts_in")
        s_rset = sem("route_consts_set")
        s_ex = sem("exp_in")
        s_exd = sem("exp_done")
        s_mask = sem("mask_ready")
        s_pre = sem("ranks_done")
        s_hot = sem("one_hots")
        s_lst = sem("lists_done")
        s_tab = sem("tables_ready")
        s_zero = sem("xg_zeroed")
        s_gn = sem("gather_index")
        s_gat = sem("gathered")
        s_xt = sem("x_transposed")
        s_xthi = sem("x_t_hi")
        s_xtlo = sem("x_t_lo")
        s_w1 = sem("w1_used")
        s_w3 = sem("w3_used")
        s_w2 = sem("w2_used")
        s_silu = sem("silu_done")
        s_hid = sem("hid_rows")
        s_htr = sem("hid_transposed")
        s_hthi = sem("hid_t_hi")
        s_htlo = sem("hid_t_lo")
        s_y = sem("y_rows")
        s_pn = sem("put_index")
        s_put = sem("y_put")
        s_yfree = sem("y_rows_free")
        s_allput = sem("all_rows_put")
        s_fg = sem("ln2_in")
        s_fh = [sem(f"final_in{t}") for t in range(NT)]
        s_fve = sem("final_var_eps")
        s_fr = sem("final_rstd")
        s_fn = sem("final_normed")
        s_fm = sem("final_scaled")
        s_fo = sem("final_rows")
        s_store = sem("stored")

        block = ctx.enter_context(nc.Block())

        def bc(ap, n=P):
            return ap.rearrange("(a d) -> a d", a=1).to_broadcast([n, ap.shape[0]])

        N_CONST = 7

        @block.sync
        def _(sp):
            def load_mixer(j):
                if j < 8:
                    s0 = 2 if j % 2 == 0 else 0
                    dst = stage[:, j % 2, :].rearrange("p (k s c) -> p k s c", k=KT, s=2)
                    for i in range(2):
                        sp.dma_start(dst[:, :, i], w_in_v[:, :, s0 + i, j // 2, :]).then_inc(s_stage[j % 2], 16)
                else:
                    n, b = divmod(j - 8, 2)
                    dst = stage[:, j % 2, :].rearrange("p (a r c) -> p a r c", a=2, r=2)
                    for i in range(2):
                        sp.dma_start(dst[:, i], w_out_v[:, b, n, i]).then_inc(s_stage[j % 2], 16)

            def x_first(t):
                sp.dma_start(hres[:, t, :], x_rows[t * P:(t + 1) * P, :]).then_inc(s_x0[t], 16)

            x_first(0)
            sp.dma_start(g_in[:], bc(ln_in_g)).then_inc(s_gin, 16)
            sp.dma_start(b_in[:], bc(ln_in_b)).then_inc(s_gin, 16)
            x_first(1)
            for j in range(CU):
                if j >= 2:
                    sp.wait_ge(s_lo, j - 1)
                load_mixer(j)
                if j < 2:
                    x_first(j + 2)
            with sp.Fori(1, NCH) as c:
                for j in range(CU):
                    sp.wait_ge(s_lo, c * CU + j - 1)
                    load_mixer(j)
            def load_expert(ex, j):
                v = (w1_v, w3_v, w2_v)[j // 2]
                kts = v.shape[2] // 2
                src = v[bass.ds(ex, 1), :, (j % 2) * kts:(j % 2 + 1) * kts, :]
                dst = staged(j)[:, 0, :].rearrange("p (k c) -> p k c", k=kts)
                sp.dma_start(dst, src.rearrange("e p k c -> p (e k) c")).then_inc(s_stage[j], 16)

            for j in range(EU):
                if j < 2:
                    sp.wait_ge(s_lo, MU - 1 + j)
                elif j == 2:
                    sp.wait_ge(s_mix, 2 * NCH * NG)
                    sp.wait_ge(s_pmhi, NCH * NG)
                elif j == 5:
                    sp.wait_ge(s_log, NT)
                load_expert(0, j)
            with sp.Fori(1, NE) as ex:
                for j in range(EU):
                    sp.wait_ge(s_lo, ex * EU + (MU - EU) + j + 1)
                    load_expert(ex, j)

            sp.wait_ge(s_lo, MU + NE * EU)
            sp.dma_start(g_2[:], bc(ln2_g[0])).then_inc(s_fg, 16)
            sp.dma_start(b_2[:], bc(ln2_b[0])).then_inc(s_fg, 16)
            sp.wait_ge(s_allput, 1)

            for t in range(NT):
                sp.dma_start(f_rows[:, t, :], sum_dram[t * P:(t + 1) * P, :]).then_inc(s_fh[t], 16)
            for t in range(NT):
                sp.wait_ge(s_fo, t + 1)
                sp.dma_start(out_rows[t * P:(t + 1) * P, :], f_rows[:, t, :]).then_inc(s_store, 16)
            sp.wait_ge(s_store, 16 * NT)

        @block.tensor
        def _(pe):
            def three(dst, w_hi, w_lo, x_hi, x_lo, start, stop):
                nc.tensor.matmul(dst, w_hi, x_hi, start=start, stop=False)
                nc.tensor.matmul(dst, w_hi, x_lo, start=False, stop=False)
                return nc.tensor.matmul(dst, w_lo, x_hi, start=False, stop=stop)

            def unit_cols(slot, lo, n):
                return [a[:, slot, lo:lo + n] for a in (ring_hi, ring_lo)]

            def section(slot, which, bank):
                for k in range(KT):
                    w = unit_cols(slot, (2 * k + which) * P, P)
                    mm = three(acc[bank][:], *w, ht_v[0][:, k, :], ht_v[1][:, k, :], k == 0, k == KT - 1)
                return mm

            def transpose_tile(rows, sem_out):
                for b in range(2):
                    for q in range(4):
                        k = 4 * b + q
                        mm = nc.tensor.transpose(tp[b][:, q, :], rows[:, k * P:(k + 1) * P], ident[:])
                    mm.then_inc(sem_out, 1)

            def tr_tile(c, t):
                pe.wait_ge(s_h, c * TPC + t + 1)
                if not (isinstance(c, int) and c == 0 and t == 0):
                    pe.wait_ge(s_trlo, (c * TPC + t) * 2)
                if t == 0 and not (isinstance(c, int) and c <= 1):
                    pe.wait_ge(s_h1tc, (c - 1) * TPC * 2)
                transpose_tile(hres[:, t, :] if isinstance(c, int) and c == 0 else hrow[:, t % 2, :], s_tr)

            def pool_map(c, g):
                if isinstance(c, int) and c == 0 and g == 0:
                    pe.wait_ge(s_pw, 2)
                    pe.wait_ge(s_const, 16 * N_CONST)
                pe.wait_ge(s_polo, c * NG + g + 1)
                if not (isinstance(c, int) and c == 0 and g == 0):
                    pe.wait_ge(s_mix, (c * NG + g) * 2)
                three(aux[:], pw_hi[:, g, :], pw_lo[:, g, :], mix_v[0][:, g, :], mix_v[1][:, g, :], True, True)\
                    .then_inc(s_pm, 1)

            def h1_tile(c, t):
                pe.wait_ge(s_h1, c * TPC + t + 1)
                if t >= 1:
                    pe.wait_ge(s_h1tc, (c * TPC + t) * 2)
                transpose_tile(hres[:, t, :], s_h1t)

            def route_tile(c, t):
                pe.wait_ge(s_h1tc, (c * TPC + t + 1) * 2)
                tile = (c * TPC + t)
                dst = logits[:, bass.ds(tile * NE, NE)]
                for k in range(KT):
                    mm = nc.tensor.matmul(dst, h1t[:, k, :], wr[:, k, :], start=(k == 0), stop=(k == KT - 1))
                mm.then_inc(s_log, 1)

            LAST = NCH - 1

            def chunk(c, first, last):
                for j in range(8):
                    g = j // 2
                    pe.wait_ge(s_lo, c * CU + j + 1)
                    if j == 0:
                        pe.wait_ge(s_trlo, (c + 1) * TPC * 2)
                    slot = j % RING1
                    for which in range(2):
                        sct = (j % 2) * 2 + which
                        if g == 0 and not first:
                            pe.wait_ge(s_res, c * 2 * TPC - TPC + sct + 1)
                        if g > 0:
                            pe.wait_ge(s_free[sct], c * NG + g)
                        section(slot, which, sct).then_inc(s_sec[sct], 1)
                    if j % 2 == 0 and g > 0:
                        pool_map(c, g - 1)
                    if not first:
                        if 3 <= j < 7:
                            route_tile(c - 1, j - 3)
                        if 2 <= j < 6:
                            h1_tile(c - 1, j - 2)
                def half(j, t, n, b):
                    for a in range(2):
                        for q in range(2):
                            k = 4 * a + 2 * b + q
                            w = [mix_v[i][:, k, t * P:(t + 1) * P] for i in range(2)]
                            xs = unit_cols(j % RING1, (2 * a + q) * 512, 512)
                            mm = three(acc[t][:], *w, *xs, b == 0 and a == 0 and q == 0, b == 1 and a == 1 and q == 1)
                    if b == 1:
                        mm.then_inc(s_out, 1)
                    return mm

                for j in range(8, 10 if last else CU):
                    n, b = divmod(j - 8, 2)
                    if j == 8:
                        if not last:
                            tr_tile(c + 1, 0)
                        pe.wait_ge(s_mix, (c * NG + 3) * 2)
                    if j == 9:
                        pe.wait_ge(s_mix, (c * NG + 4) * 2)
                    pe.wait_ge(s_lo, c * CU + j + 1)
                    for t in range(TPC):
                        if j == 8:
                            pe.wait_ge(s_free[t], (c + 1) * NG)
                        if j == 10:
                            pe.wait_ge(s_res, c * 2 * TPC + t + 1)
                        mm = half(j, t, n, b)
                        if j == 8 and t == 1:
                            pool_map(c, 3)
                    if b == 0:
                        mm.then_inc(s_used, 1)
                    if not last and j < CU - 1:
                        tr_tile(c + 1, j - 7)
                if last:
                    pe.wait_ge(s_lo, c * CU + CU)
                    for t in range(TPC):
                        pe.wait_ge(s_res, c * 2 * TPC + t + 1)
                        half(10, t, 1, 0)
                        half(11, t, 1, 1)

            pe.wait_ge(s_cset, 1)
            for t in range(TPC):
                tr_tile(0, t)
            chunk(0, True, False)
            with pe.Fori(1, NCH - 1) as c:
                chunk(c, False, False)
            chunk(LAST, False, True)
            def h1_last(t):
                pe.wait_ge(s_h1, LAST * TPC + t + 1)
                if t < 2:
                    pe.wait_ge(s_res, NCH * 2 * TPC)
                else:
                    pe.wait_ge(s_h1tc, (LAST * TPC + t - 1) * 2)
                for b in range(2):
                    for q in range(4):
                        k = 4 * b + q
                        mm = nc.tensor.transpose(last_banks[t % 2][b][:, q, :], hres[:, t, k * P:(k + 1) * P], ident[:])
                    mm.then_inc(s_h1t, 1)

            def route_last(t):
                pe.wait_ge(s_h1tc, (LAST * TPC + t + 1) * 2)
                tile = LAST * TPC + t
                for k in range(KT):
                    mm = nc.tensor.matmul(logits[:, tile * NE:(tile + 1) * NE], (h1t, h1t_b)[t % 2][:, k, :], wr[:, k, :],
                                          start=(k == 0), stop=(k == KT - 1))
                mm.then_inc(s_log, 1)

            h1_last(0)
            for t in range(TPC):
                if t + 1 < TPC:
                    h1_last(t + 1)
                route_last(t)

            pe.wait_ge(s_rset, 3)
            pe.wait_ge(s_mask, 1)
            flat = mask[:].rearrange("p t e -> p (t e)")
            nc.tensor.matmul(acc[0][:, 0:256], upper[:], flat, start=True, stop=True)
            nc.tensor.matmul(acc[1][:, 0:256], ones[:], flat, start=True, stop=True).then_inc(s_pre, 1)
            for k in range(2):
                for t in range(NT):
                    if t % HOT_T == 0:
                        pe.wait_ge(s_hot, 2 * k + t // HOT_T + 1)
                    mm = nc.tensor.matmul(acc[2][:, 0:2 * NBP], hot_r[:, k, t, :],
                                          hot_b[:, k, t].rearrange("p v b -> p (v b)"),
                                          start=k == 0 and t == 0, stop=k == 1 and t == NT - 1)
            mm.then_inc(s_lst, 1)

            def x_tile(b):
                pe.wait_ge(s_gat, b * 16 + 16)
                if not (isinstance(b, int) and b == 0):
                    pe.wait_ge(s_xtlo, b * 2)
                transpose_tile(xg[:], s_xt)

            def up(b, base, e_of, which, used):
                for h in range(2):
                    pe.wait_ge(s_lo, e_of * EU + MU + 2 * which + h + 1)
                    slot = (base + (2 * which + h)) % RING
                    for q in range(4):
                        k = 4 * h + q
                        xs = [a[:, bass.ds(slot, 1), q * 512:(q + 1) * 512].rearrange("p u c -> p (u c)")
                              for a in (ring_hi, ring_lo)]
                        mm = three(acc[which][:], xt_hi[:, k, :], xt_lo[:, k, :], *xs,
                                   k == 0, k == KT - 1)
                mm.then_inc(used, 1)

            def down(base, e_of):
                for h in range(2):
                    pe.wait_ge(s_lo, e_of * EU + MU + 4 + h + 1)
                    slot = (base + (4 + h)) % RING
                    for q in range(2):
                        k = 2 * h + q
                        for n in range(2):
                            o = q * 1024 + n * 512
                            xs = [a[:, bass.ds(slot, 1), o:o + 512].rearrange("p u c -> p (u c)")
                                  for a in (ring_hi, ring_lo)]
                            mm = three(acc[2 + n][:], ht_hi[:, k, :], ht_lo[:, k, :], *xs,
                                       k == 0, k == FT - 1)
                mm.then_inc(s_w2, 1)

            def hid_tile(b):
                pe.wait_ge(s_hid, b + 1)
                if not (isinstance(b, int) and b == 0):
                    pe.wait_ge(s_htlo, b)
                for q in range(FT):
                    mm = nc.tensor.transpose(aux[:, q * P:(q + 1) * P], hid[:, q * P:(q + 1) * P], ident[:])
                mm.then_inc(s_htr, 1)

            pe.wait_ge(s_tab, 1)
            nb = pe.value_load(nblocks[0:1, 0:1], min_val=NE, max_val=NB)
            pe.sem_inc(s_w2, 1)
            x_tile(0)
            pe.wait_ge(s_xtlo, 2)
            up(0, 0, 0, 0, s_w1)
            up(0, 0, 0, 1, s_w3)
            x_tile(1)
            hid_tile(0)
            with pe.Fori(1, nb) as b:
                base = pe.value_load(table[0:1, 0, bass.ds(b, 1)], min_val=0, max_val=RING - 2)
                e_of = pe.value_load(table[0:1, 1, bass.ds(b, 1)], min_val=0, max_val=NE - 1)
                pe.wait_ge(s_xtlo, b * 2 + 2)
                pe.wait_ge(s_silu, b)
                up(b, base, e_of, 0, s_w1)
                pe.wait_ge(s_hid, b)
                up(b, base, e_of, 1, s_w3)
                x_tile(b + 1)
                pbase = pe.value_load(table[0:1, 0, bass.ds(b - 1, 1)], min_val=0, max_val=RING - 2)
                pe_of = pe.value_load(table[0:1, 1, bass.ds(b - 1, 1)], min_val=0, max_val=NE - 1)
                pe.wait_ge(s_htlo, b)
                pe.wait_ge(s_y, b)
                down(pbase, pe_of)
                hid_tile(b)
            lbase = pe.value_load(table[0:1, 0, bass.ds(nb - 1, 1)], min_val=0, max_val=RING - 2)
            pe.wait_ge(s_htlo, nb)
            pe.wait_ge(s_y, nb)
            down(lbase, NE - 1)

        @block.scalar
        def _(act):
            def split_hi(slot_in, landed, slot):
                act.wait_ge(s_stage[slot_in], landed)
                nc.scalar.copy(ring_hi[:, bass.ds(slot, 1), :], staged(slot_in)).then_inc(s_hi, 1)

            def split_hi_expert(ex, j, slot):
                split_hi(j, (ex + 1) * 16 + (MU // 2 * 32 if j < 2 else 0), slot)

            def unit_ahead(c, j, last):
                ja = j + RING1 - 1
                if ja >= CU and last:
                    return
                slot_in = ja % 2
                landed = (c * (CU // 2) + (ja // 2) + 1) * 32
                if not (isinstance(c, int) and c == 0 and j == 0):
                    if j == 0:
                        act.wait_ge(s_out, c * 2 * TPC)
                    elif j < 9:
                        q = (j - 1) // 2
                        act.wait_ge(s_sec[3 if (j - 1) % 2 else 1], c * NG + q + 1)
                    elif j == 10:
                        act.wait_ge(s_out, c * 2 * TPC + TPC)
                    else:
                        act.wait_ge(s_used, c * 2 + (1 if j == 9 else 2))
                split_hi(slot_in, landed, ja % RING1)

            def tr_hi(c, t):
                for b in range(2):
                    act.wait_ge(s_tr, (c * TPC + t) * 2 + b + 1)
                    nc.scalar.copy(ht_v[0][:, 4 * b:4 * b + 4, t * P:(t + 1) * P], tp[b][:]).then_inc(s_trhi, 1)

            def pool_mix_hi(c, g):
                act.wait_ge(s_pm, c * NG + g + 1)
                nc.scalar.activation(mix_v[0][:, g, :], aux[:], ACT.Copy, scale=ps[:, g:g + 1]).then_inc(s_pmhi, 1)

            def conv_mix_hi(c, g):
                act.wait_ge(s_cv, c * NG + g + 1)
                nc.scalar.copy(mix_v[0][:, NG + g, :], cacc[:]).then_inc(s_cvhi, 1)

            def h1t_copy(c, t):
                for b in range(2):
                    act.wait_ge(s_h1t, (c * TPC + t) * 2 + b + 1)
                    nc.scalar.copy(h1t[:, 4 * b:4 * b + 4, :], tp[b][:]).then_inc(s_h1tc, 1)

            def alpha_h1(c, t):
                act.wait_ge(s_h1out[t], c * 16 + 16)
                act.wait_ge(s_h1t, (c * TPC + t + 1) * 2)
                nc.scalar.mul(hres[:, t, :], hres[:, t, :], ALPHA).then_inc(s_ah, 1)
                act.wait_ge(s_ah, c * TPC + t + 1)
                act.dma_start(sum_dram[bass.ds((c * TPC + t) * P, P), :], hres[:, t, :]).then_inc(s_ahout[t], 16)

            def res_load(c, t):
                act.wait_ge(s_ahout[t], c * 16)
                act.wait_ge(s_h0out[t], c * 16)
                act.dma_start(hres[:, t, :], h0_dram[bass.ds((c * TPC + t) * P, P), :]).then_inc(s_hres[t], 16)

            def chunk(c, first, last):
                for j in range(CU):
                    if j == 9:
                        pool_mix_hi(c, 3)
                    unit_ahead(c, j, last)
                    g = j // 2
                    if not first and 3 <= j < 7:
                        h1t_copy(c - 1, j - 3)
                    if not first and 4 <= j < 8:
                        alpha_h1(c - 1, j - 4)
                    if not first and 5 <= j < 9:
                        res_load(c, j - 5)
                    if j < 8 and j % 2 == 0:
                        if g > 0:
                            conv_mix_hi(c, g - 1)
                        if not (first and g == 0):
                            act.wait_ge(s_cv, c * NG + g)
                        act.wait_ge(s_sec[1], c * NG + g + 1)
                        nc.scalar.copy(zext[:, 2:], acc[1][:]).then_inc(s_free[1], 1)
                    if j < 8 and j % 2 == 1:
                        if g > 0:
                            pool_mix_hi(c, g - 1)
                        act.wait_ge(s_z, c * NG + g + 1)
                        if not (first and g == 0):
                            act.wait_ge(s_mix, (c * NG + g) * 2 - 1)
                        nc.scalar.activation(cacc[:], zext[:, 2:], ACT.Identity, scale=cw[:, 2, g:g + 1],
                                             bias=cb[:, g:g + 1]).then_inc(s_zt, 1)
                        act.wait_ge(s_sec[2], c * NG + g + 1)
                        if not (first and g == 0):
                            act.wait_ge(s_pool, c * NG + g)
                        nc.scalar.copy(vext[:, HIST:], acc[2][:]).then_inc(s_free[2], 1)
                        act.wait_ge(s_pool, c * NG + g + 1)
                        nc.scalar.copy(mix_v[0][:, g, :], sum_a[:, HIST:]).then_inc(s_pohi, 1)
                    if j == 8:
                        conv_mix_hi(c, 3)
                        if not last:
                            tr_hi(c + 1, 0)
                    if 9 <= j and not last:
                        tr_hi(c + 1, j - 8)

            for t in range(TPC):
                tr_hi(0, t)
                if t < 2:
                    split_hi(t, 32, t)
            split_hi(0, 64, 2)
            act.wait_ge(s_const, 16 * N_CONST)
            nc.scalar.copy(pw_hi[:], pw_raw).then_inc(s_pw, 1)
            chunk(0, True, False)
            with act.Fori(1, NCH - 1) as c:
                chunk(c, False, False)
            chunk(NCH - 1, False, True)
            act.wait_ge(s_out, NCH * 2 * TPC)
            for t in range(TPC):
                for b in range(2):
                    act.wait_ge(s_h1t, ((NCH - 1) * TPC + t) * 2 + b + 1)
                    if t >= 2:
                        act.wait_ge(s_log, (NCH - 1) * TPC + t - 1)
                    nc.scalar.copy((h1t, h1t_b)[t % 2][:, 4 * b:4 * b + 4, :], last_banks[t % 2][b][:])\
                        .then_inc(s_h1tc, 1)
            split_hi_expert(0, 0, 0)
            alpha_h1(NCH - 1, 0)
            act.wait_ge(s_ex, 1)
            nc.scalar.activation(prob[:], t_a[:], ACT.Exp).then_inc(s_exd, 1)
            for t in range(1, TPC):
                split_hi_expert(0, t, t)
                alpha_h1(NCH - 1, t)
            for j in range(TPC, EU):
                split_hi_expert(0, j, j)

            act.wait_ge(s_tab, 1)
            nb = act.value_load(nblocks[0:1, 0:1], min_val=NE, max_val=NB)

            def x_hi(b):
                for h in range(2):
                    act.wait_ge(s_xt, b * 2 + h + 1)
                    nc.scalar.copy(xt_hi[:, 4 * h:4 * h + 4, :], tp[h][:]).then_inc(s_xthi, 1)

            def hid_hi(b):
                act.wait_ge(s_htr, b + 1)
                nc.scalar.copy(ht_hi[:], aux[:].rearrange("p (k t) -> p k t", t=P)).then_inc(s_hthi, 1)

            def silu(b):
                act.wait_ge(s_w1, b + 1)
                if not (isinstance(b, int) and b == 0):
                    act.wait_ge(s_hid, b)
                nc.scalar.activation(act_a[:], acc[0][:], ACT.Silu).then_inc(s_silu, 1)

            def y_rows(b):
                act.wait_ge(s_w2, b + 2)
                act.wait_ge(s_yfree, b + 1)
                for n in range(2):
                    ins = nc.scalar.copy(yrow[:, n * 512:(n + 1) * 512], acc[2 + n][:])
                ins.then_inc(s_y, 1)

            def next_units(e_of, base, js):
                for j in js:
                    split_hi_expert(e_of + 1, j, (base + (EU + j)) % RING)

            def turn(b, first):
                base = act.value_load(table[0:1, 0, bass.ds(b, 1)], min_val=0, max_val=RING - 2)
                e_of = act.value_load(table[0:1, 1, bass.ds(b, 1)], min_val=0, max_val=NE - 1)
                fb = act.value_load(table[0:1, 2, bass.ds(b, 1)], min_val=0, max_val=NB)
                sp_ = act.value_load(table[0:1, 3, bass.ds(b, 1)], min_val=0, max_val=1)
                if not first:
                    hid_hi(b - 1)
                with act.If(sp_ > 0):
                    act.wait_ge(s_w2, fb)
                    next_units(e_of, base, (0, 1))
                silu(b)
                with act.If(sp_ > 0):
                    next_units(e_of, base, (2, 3))
                act.wait_ge(s_w3, b + 1)
                x_hi(b + 1)
                with act.If(sp_ > 0):
                    next_units(e_of, base, (4, 5))
                if not first:
                    y_rows(b - 1)

            x_hi(0)
            turn(0, True)
            with act.Fori(1, nb) as b:
                turn(b, False)
            hid_hi(nb - 1)
            y_rows(nb - 1)

            for t in range(NT):
                i = t
                act.wait_ge(s_fr, t + 1)
                act.wait_ge(s_fm, t + 1)
                nc.scalar.mul(f_rows[:, i, :], f_rows[:, i, :], frstd[:, i:i + 1]).then_inc(s_fn, 1)

        @block.vector
        def _(dve):
            ch = Chain(dve, s_dve)
            V = nc.vector

            def split_lo(slot_in, count, slot):
                dve.wait_ge(s_hi, count)
                hi, lo = (a[:, bass.ds(slot, 1), :] for a in (ring_hi, ring_lo))
                V.tensor_tensor(lo, staged(slot_in), hi.bitcast(F32), ALU.subtract).then_inc(s_lo, 1)

            def unit_ahead(c, j, last):
                ja = j + RING1 - 1
                if ja >= CU and last:
                    return
                split_lo(ja % 2, c * CU + ja + 1, ja % RING1)

            def norm_stats(rows):
                V.bn_stats(stats[:, 0, :], rows[:, 0:512])
                ch.link(V.bn_stats(stats[:, 1, :], rows[:, 512:1024]))
                carry(dve, s_dve_past)
                ch.link(V.bn_aggr(mv[:], stats[:].rearrange("p a b -> p (a b)")))
                V.tensor_scalar(vareps[:], mv[:, 1:2], EPS, None, ALU.add).then_inc(s_ve, 1)

            def norm_rows(n, rows, g, b, done):
                ch.link(V.scalar_tensor_tensor(out=rows, in0=rows, scalar=mv[:, 0:1], in1=g, op0=ALU.subtract, op1=ALU.mult))
                dve.wait_ge(s_rstd, n + 1)
                V.scalar_tensor_tensor(out=rows, in0=rows, scalar=rstd[:], in1=b, op0=ALU.mult, op1=ALU.add).then_inc(done, 1)

            def ln_h(c, t, n):
                if isinstance(c, int) and c == 0:
                    rows = hres[:, t, :]
                    dve.wait_ge(s_x0[t], 16)
                else:
                    rows = hrow[:, t % 2, :]
                    dve.wait_ge(s_x[t % 2], ((c - 1) * 2 + t // 2 + 1) * 16)
                norm_stats(rows)
                if isinstance(c, int) and c == 0 and t == 0:
                    dve.wait_ge(s_gin, 32)
                norm_rows(n, rows, g_in[:], b_in[:], s_h)

            def ln_h1(c, t, n):
                rows = hres[:, t, :]
                dve.wait_ge(s_res, c * 2 * TPC + TPC + t + 1)
                norm_stats(rows)
                norm_rows(n, rows, g_1[:], b_1[:], s_h1)

            def tr_lo(c, t):
                for b in range(2):
                    dve.wait_ge(s_trhi, (c * TPC + t) * 2 + b + 1)
                    cols = (slice(None), slice(4 * b, 4 * b + 4), slice(t * P, (t + 1) * P))
                    V.tensor_tensor(ht_v[1][cols], tp[b][:], ht_v[0][cols].bitcast(F32), ALU.subtract).then_inc(s_trlo, 1)

            def z_rows(c, g):
                dve.wait_ge(s_sec[0], c * NG + g + 1)
                dve.wait_ge(s_free[1], c * NG + g + 1)
                ch.mark(V.tensor_copy(zext[:, 0:2], zhist[:, g, :]))
                V.tensor_tensor(zext[:, 2:], zext[:, 2:], acc[0][:], ALU.mult).then_inc(s_z, 1)
                dve.wait_ge(s_z, c * NG + g + 1)
                V.tensor_copy(zhist[:, g, :], zext[:, CHUNK:]).then_inc(s_free[0], 1)

            def pool_rows(c, g):
                w = WINDOWS[g]
                n = HIST + CHUNK
                dve.wait_ge(s_free[2], c * NG + g + 1)
                if not (isinstance(c, int) and c == 0 and g == 0):
                    dve.wait_ge(s_pohi, c * NG + g)
                ch.link(V.tensor_copy(vext[:, 0:HIST], vhist[:, g, :]))
                src, k = vext, 1
                bufs = [sum_b, sum_a]
                levels = w.bit_length() - 1
                if levels % 2 == 0:
                    bufs = bufs[::-1]
                for i in range(levels):
                    dst = bufs[i % 2]
                    lo = 2 * k - 1
                    ch.link(V.tensor_tensor(dst[:, lo:n], src[:, lo:n], src[:, lo - k:n - k], ALU.add))
                    src, k = dst, 2 * k
                ch.mark(V.scalar_tensor_tensor(out=sum_a[:, 2 * HIST:], in0=src[:, 2 * HIST:], scalar=1.0 / w,
                                               in1=vext[:, 2 * HIST:], op0=ALU.mult, op1=ALU.subtract))
                ch.link(V.tensor_tensor(sum_a[:, HIST:2 * HIST], src[:, HIST:2 * HIST], edge[:, g, :], ALU.mult))
                ch.link(V.tensor_tensor(sum_a[:, HIST:2 * HIST], sum_a[:, HIST:2 * HIST], vext[:, HIST:2 * HIST], ALU.subtract))
                V.tensor_copy(vhist[:, g, :], vext[:, CHUNK:]).then_inc(s_pool, 1)

            def conv_rows(c, g):
                dve.wait_ge(s_zt, c * NG + g + 1)
                ch.link(V.scalar_tensor_tensor(out=cacc[:], in0=zext[:, 1:1 + CHUNK], scalar=cw[:, 1, g:g + 1],
                                               in1=cacc[:], op0=ALU.mult, op1=ALU.add))
                ch.link(V.scalar_tensor_tensor(out=cacc[:], in0=zext[:, 0:CHUNK], scalar=cw[:, 0, g:g + 1],
                                               in1=cacc[:], op0=ALU.mult, op1=ALU.add))

            def pooled_split(c, g):
                dve.wait_ge(s_pohi, c * NG + g + 1)
                V.tensor_tensor(mix_v[1][:, g, :], sum_a[:, HIST:], mix_v[0][:, g, :].bitcast(F32),
                                ALU.subtract).then_inc(s_polo, 1)

            def gate_rows(c, g):
                dve.wait_ge(s_sec[3], c * NG + g + 1)
                V.tensor_tensor(cacc[:], cacc[:], acc[3][:], ALU.mult).then_inc(s_cv, 1)


            def conv_lo(c, g):
                dve.wait_ge(s_cvhi, c * NG + g + 1)
                V.tensor_tensor(mix_v[1][:, NG + g, :], cacc[:], mix_v[0][:, NG + g, :].bitcast(F32),
                                ALU.subtract).then_inc(s_mix, 1)

            def pool_mix_lo(c, g):
                dve.wait_ge(s_pmhi, c * NG + g + 1)
                V.scalar_tensor_tensor(out=mix_v[1][:, g, :], in0=aux[:], scalar=ps[:, g:g + 1],
                                       in1=mix_v[0][:, g, :].bitcast(F32), op0=ALU.mult,
                                       op1=ALU.subtract).then_inc(s_mix, 1)

            def residual(c, n, t):
                if n == 0:
                    if isinstance(c, int) and c == 0:
                        dve.wait_ge(s_h, t + 1)
                    else:
                        dve.wait_ge(s_hres[t], c * 16)
                dve.wait_ge(s_out, c * 2 * TPC + n * TPC + t + 1)
                cols = hres[:, t, n * 512:(n + 1) * 512]
                V.scalar_tensor_tensor(out=cols, in0=cols, scalar=ALPHA, in1=acc[t][:], op0=ALU.mult,
                                       op1=ALU.add).then_inc(s_res, 1)

            def chunk(c, first, last):
                n = [TPC if first else (c - 1) * 8 + 2 * TPC]

                def nth():
                    n[0] = n[0] + 1
                    return n[0] - 1
                for j in range(CU):
                    if j == 9:
                        pool_mix_lo(c, 3)
                    if j == 10:
                        for t in range(TPC):
                            residual(c, 0, t)
                    unit_ahead(c, j, last)
                    g = j // 2
                    if j < 8 and j % 2 == 0:
                        z_rows(c, g)
                        if g > 0:
                            conv_lo(c, g - 1)
                    if j < 8 and j % 2 == 1:
                        if g > 0:
                            pool_mix_lo(c, g - 1)
                        pool_rows(c, g)
                        conv_rows(c, g)
                        pooled_split(c, g)
                        if g == 3 and first:
                            for gg, w in enumerate(WINDOWS):
                                ins = V.memset(edge[:, gg, :], 1.0 / w)
                            ch.link(ins)
                    if not first and j < 4:
                        ln_h1(c - 1, j, nth())
                    if j < 8 and j % 2 == 1:
                        gate_rows(c, g)
                    if not last:
                        if j in (5, 7):
                            ln_h(c + 1, (j - 5) // 2, nth())
                        if j == 8:
                            conv_lo(c, 3)
                            tr_lo(c + 1, 0)
                        if j == 9:
                            ln_h(c + 1, 2, nth())
                            tr_lo(c + 1, 1)
                        if j == 10:
                            ln_h(c + 1, 3, nth())
                            tr_lo(c + 1, 2)
                        if j == 11:
                            tr_lo(c + 1, 3)
                            for t in range(TPC):
                                residual(c, 1, t)
                    else:
                        if j == 8:
                            conv_lo(c, 3)
                        if j == 11:
                            for t in range(TPC):
                                residual(c, 1, t)
                                ln_h1(c, t, 8 * NCH - TPC + t)

            ln_h(0, 0, 0)
            ln_h(0, 1, 1)
            for t in range(TPC):
                tr_lo(0, t)
                if t < 2:
                    ln_h(0, t + 2, t + 2)
                if t == 0:
                    split_lo(0, 1, 0)
            for j in range(1, RING1 - 1):
                split_lo(j % 2, j + 1, j)
            dve.wait_ge(s_pw, 1)
            V.tensor_tensor(pw_lo[:], pw_raw, pw_hi[:].bitcast(F32), ALU.subtract).then_inc(s_pw, 1)
            dve.wait_ge(s_cset, 2)
            for g, w in enumerate(WINDOWS):
                ins = V.tensor_scalar(edge[:, g, :], edge[:, g, :], float(w), None, ALU.min)
            ch.link(ins)
            ch.link(V.reciprocal(edge[:], edge[:]))
            chunk(0, True, False)
            with dve.Fori(1, NCH - 1) as c:
                ch.enter(c - 1, DVE_PER_CHUNK)
                chunk(c, False, False)
                ch.leave(NCH - 2)
            chunk(NCH - 1, False, True)
            dve.wait_ge(s_log, NT)
            dve.wait_ge(s_rset, 6)
            dve.wait_ge(s_rin, 16)
            lg = logits[:, 0:NT * NE].rearrange("p (t e) -> p t e", e=NE)

            def over_e(a):
                return a[:].unsqueeze(2).to_broadcast(NTE)

            def tt(out, a, b, op):
                ch.link(V.tensor_tensor(out, a, b, op))

            def red(out, a, op):
                ch.link(V.tensor_reduce(out, a, AX.X, op))

            iota = iota_e[:].unsqueeze(1).to_broadcast(NTE)
            red(row_a[:], lg, ALU.max)
            ins = V.tensor_tensor(t_a[:], lg, over_e(row_a), ALU.subtract)
            ins.then_inc(s_ex, 1)
            dve.wait_ge(s_exd, 1)
            red(row_b[:], prob[:], ALU.add)
            ch.link(V.reciprocal(row_b[:], row_b[:]))
            tt(prob[:], prob[:], over_e(row_b), ALU.mult)
            tt(sel[:], prob[:], bias_bc[:].unsqueeze(1).to_broadcast(NTE), ALU.add)
            s4 = sel[:].rearrange("p t (g i) -> p (t g) i", i=EPG)
            V.tensor_tensor(gs_a[:], s4[:, :, 0], s4[:, :, 1], ALU.max)
            V.tensor_tensor(gs_b[:], s4[:, :, 0], s4[:, :, 1], ALU.min)
            V.tensor_tensor(gs_c[:], s4[:, :, 2], s4[:, :, 3], ALU.max)
            tt(gs_d[:], s4[:, :, 2], s4[:, :, 3], ALU.min)
            tt(gs_b[:], gs_b[:], gs_d[:], ALU.max)
            tt(gs_d[:], gs_a[:], gs_c[:], ALU.min)
            tt(gs_b[:], gs_b[:], gs_d[:], ALU.max)
            tt(gs_a[:], gs_a[:], gs_c[:], ALU.max)
            tt(gs_a[:], gs_a[:], gs_b[:], ALU.add)

            def first_hot(vals, shape, top, eq, hot, iota_ap, far):
                over = lambda a: a[:].unsqueeze(2).to_broadcast(shape)
                red(top[:], vals, ALU.max)
                tt(eq, vals, over(top), ALU.is_equal)
                ch.link(V.scalar_tensor_tensor(out=eq, in0=eq, scalar=-far, in1=iota_ap, op0=ALU.mult, op1=ALU.add))
                red(top[:], eq, ALU.min)
                tt(hot, eq, over(top), ALU.is_equal)

            g3 = [P, NT, NEG]
            gv = lambda a: a[:].rearrange("p (t g) -> p t g", g=NEG)
            first_hot(gv(gs_a), g3, row_a, gv(gs_b), gv(gs_c), iota_e[:, 0:NEG].unsqueeze(1).to_broadcast(g3), 64.0)
            ch.link(V.tensor_scalar(gs_c[:], gs_c[:], BIG, -BIG, ALU.mult, ALU.add))
            tt(t_b[:].rearrange("p t (g i) -> p (t g) i", i=EPG), s4,
               gs_c[:].unsqueeze(2).to_broadcast([P, NT * NEG, EPG]), ALU.add)
            first_hot(t_b[:], NTE, row_a, t_c[:], oh1[:], iota, 64.0)
            ch.link(V.scalar_tensor_tensor(out=t_b[:], in0=oh1[:], scalar=-3 * BIG, in1=t_b[:], op0=ALU.mult, op1=ALU.add))
            first_hot(t_b[:], NTE, row_a, t_c[:], oh2[:], iota, 64.0)
            V.tensor_tensor(mask[:], oh1[:], oh2[:], ALU.add).then_inc(s_mask, 1)
            tt(t_c[:], oh1[:], prob[:], ALU.mult)
            tt(t_d[:], oh2[:], prob[:], ALU.mult)
            red(row_a[:], t_c[:], ALU.add)
            red(row_b[:], t_d[:], ALU.add)
            tt(row_c[:], row_a[:], row_b[:], ALU.add)
            ch.link(V.reciprocal(row_c[:], row_c[:]))
            tt(gates[:, 0, :], row_a[:], row_c[:], ALU.mult)
            tt(gates[:, 1, :], row_b[:], row_c[:], ALU.mult)
            dve.wait_ge(s_pre, 1)
            before, count = (acc[i][:, 0:NT * NE].rearrange("p (t e) -> p t e", e=NE) for i in range(2))
            ch.link(V.tensor_copy(by_e[:], count.rearrange("p t e -> p e t")))
            ch.link(V.tensor_tensor_scan(*(a[:].rearrange("p e t -> p (e t)") for a in (sums, carries, by_e)), 0.0,
                                         ALU.mult, ALU.add))
            upto = sums[:].rearrange("p e t -> p t e")
            ch.mark(V.tensor_copy(cnt[:], sums[:, :, NT - 1]))
            tt(t_a[:], upto, by_e[:].rearrange("p e t -> p t e"), ALU.subtract)
            tt(t_a[:], t_a[:], before, ALU.add)
            tt(over[:], cnt[:].unsqueeze(2).to_broadcast([P, NE, NE]),
               iota_k[:].unsqueeze(1).to_broadcast([P, NE, NE]), ALU.is_gt)
            red(nblk[:], over[:], ALU.add)
            ch.link(V.tensor_scalar(nblk[:], nblk[:], 1.0, None, ALU.max))
            ch.link(V.tensor_tensor_scan(end[:], ones[:, 0:NE], nblk[:], 0.0, ALU.mult, ALU.add))
            tt(start[:], end[:], nblk[:], ALU.subtract)
            ch.link(V.tensor_scalar(cnt[:], start[:], float(P), None, ALU.mult))
            tt(t_a[:], t_a[:], cnt[:].unsqueeze(1).to_broadcast(NTE), ALU.add)
            tt(t_b[:], t_a[:], oh1[:], ALU.mult)
            tt(t_c[:], t_a[:], oh2[:], ALU.mult)
            red(slot_f[:, 0, :], t_b[:], ALU.add)
            red(slot_f[:, 1, :], t_c[:], ALU.add)
            ch.link(V.tensor_copy(slot_i[:], slot_f[:]))
            ch.link(V.tensor_scalar(blk_i[:], slot_i[:], 7, None, ALU.logical_shift_right))
            ch.link(V.tensor_scalar(rem_i[:], slot_i[:], P - 1, None, ALU.bitwise_and))
            ch.link(V.tensor_copy(blk_f[:], blk_i[:]))
            ch.link(V.tensor_copy(rem_f[:], rem_i[:]))
            for t in range(TPC):
                dve.wait_ge(s_ahout[t], 16 * NCH)
            HOTB, HOTR = [P, NT, NBP], [P, HOT_T, P]
            for k in range(2):
                def per_tile(a, shape):
                    return a.unsqueeze(2).to_broadcast(shape)

                tt(eq_b, iota_b[:, 0:NBP].unsqueeze(1).to_broadcast(HOTB), per_tile(blk_f[:, k, :], HOTB), ALU.is_equal)
                V.tensor_tensor(hot_b[:, k, :, 0, :], eq_b, per_tile(dest[:, k, :], HOTB), ALU.mult)
                ch.mark(V.tensor_tensor(hot_b[:, k, :, 1, :], eq_b, per_tile(gates[:, k, :], HOTB), ALU.mult))
                for i in range(NT // HOT_T):
                    ts = slice(i * HOT_T, (i + 1) * HOT_T)
                    V.tensor_tensor(hot_r[:, k, ts, :], iota_p[:].unsqueeze(1).to_broadcast(HOTR),
                                    per_tile(rem_f[:, k, ts], HOTR), ALU.is_equal).then_inc(s_hot, 1)
                ch.need(ch.n)
            B3 = [P, NBP + 1, NE]
            tt(tb_a[:], end[:].unsqueeze(1).to_broadcast(B3), iota_b[:].unsqueeze(2).to_broadcast(B3), ALU.is_le)
            red(f_e[:], tb_a[:], ALU.add)
            ch.link(V.tensor_scalar(f_e[:], f_e[:], float(NE - 1), None, ALU.min))
            ch.mark(V.tensor_copy(table[:, 1, :], f_e[:, 0:NBP]))
            tt(f_next[:], f_e[:, 0:NBP], f_e[:, 1:], ALU.not_equal)
            ch.mark(V.tensor_copy(table[:, 3, :], f_next[:]))
            tt(f_t[:, 1:], f_next[:, 0:NBP - 1], iota_b[:, 2:NBP + 1], ALU.mult)
            ch.link(V.memset(f_t[:, 0:1], 1.0))
            ch.link(V.tensor_tensor_scan(f_first[:], ones[:, 0:NBP], f_t[:], 0.0, ALU.mult, ALU.max))
            ch.mark(V.tensor_copy(table[:, 2, :], f_first[:]))
            ch.link(V.tensor_scalar(f_t[:], f_e[:, 0:NBP], float(EU), None, ALU.mult))
            ch.link(V.tensor_copy(table[:, 0, :], f_t[:]))
            ch.link(V.tensor_scalar(table[:, 0, :], table[:, 0, :], RING - 1, None, ALU.bitwise_and))
            dve.wait_ge(s_lst, 1)
            v = acc[2][:, 0:NBP]
            ch.link(V.tensor_scalar(f_t[:], v, 0.5, OOB, ALU.is_lt, ALU.mult))
            ch.link(V.scalar_tensor_tensor(out=f_t[:], in0=v, scalar=-1.0, in1=f_t[:], op0=ALU.add, op1=ALU.add))
            ch.link(V.tensor_copy(token[:], f_t[:]))
            ch.link(V.tensor_copy(gate[:], acc[2][:, NBP:2 * NBP]))
            ch.link(V.tensor_copy(nblocks[:, 0:1], end[:, NE - 1:NE]))
            ch.link(V.tensor_scalar(nblocks[:, 1:2], end[:, NE - 1:NE], -1.0, None, ALU.add))
            V.tensor_scalar(nblocks[:, 2:3], end[:, NE - 1:NE], -2.0, None, ALU.add).then_inc(s_tab, 1)

            dve.wait_ge(s_tab, 1)
            nb = dve.value_load(nblocks[0:1, 0:1], min_val=NE, max_val=NB)

            def x_lo(b):
                for h in range(2):
                    dve.wait_ge(s_xthi, b * 2 + h + 1)
                    V.tensor_tensor(xt_lo[:, 4 * h:4 * h + 4, :], tp[h][:], xt_hi[:, 4 * h:4 * h + 4, :].bitcast(F32),
                                    ALU.subtract).then_inc(s_xtlo, 1)

            def hid_rows(b):
                dve.wait_ge(s_silu, b + 1)
                dve.wait_ge(s_w3, b + 1)
                if not (isinstance(b, int) and b == 0):
                    dve.wait_ge(s_htr, b)
                col = gate[:, bass.ds(b, 1)]
                V.scalar_tensor_tensor(out=hid[:], in0=act_a[:], scalar=col, in1=acc[1][:], op0=ALU.mult,
                                       op1=ALU.mult).then_inc(s_hid, 1)

            def hid_lo(b):
                dve.wait_ge(s_hthi, b + 1)
                V.tensor_tensor(ht_lo[:], aux[:].rearrange("p (k t) -> p k t", t=P), ht_hi[:].bitcast(F32),
                                ALU.subtract).then_inc(s_htlo, 1)

            def next_units(e_of, base, js):
                for j in js:
                    split_lo(j, e_of * EU + MU + EU + j + 1, (base + (EU + j)) % RING)

            def turn(b, first):
                base = dve.value_load(table[0:1, 0, bass.ds(b, 1)], min_val=0, max_val=RING - 2)
                e_of = dve.value_load(table[0:1, 1, bass.ds(b, 1)], min_val=0, max_val=NE - 1)
                sp_ = dve.value_load(table[0:1, 3, bass.ds(b, 1)], min_val=0, max_val=1)
                if not first:
                    hid_lo(b - 1)
                with dve.If(sp_ > 0):
                    next_units(e_of, base, (0, 1, 2, 3))
                hid_rows(b)
                x_lo(b + 1)
                with dve.If(sp_ > 0):
                    next_units(e_of, base, (4, 5))

            x_lo(0)
            dve.wait_ge(s_lo, MU + EU)
            turn(0, True)
            with dve.Fori(1, nb) as b:
                turn(b, False)
            hid_lo(nb - 1)

            def final_stats(t):
                i = t
                dve.wait_ge(s_fh[i], 16)
                V.bn_stats(fstats[:, 0, :], f_rows[:, i, 0:512])
                ch.link(V.bn_stats(fstats[:, 1, :], f_rows[:, i, 512:1024]))
                ch.link(V.bn_aggr(fmv[:, i, :], fstats[:].rearrange("p a b -> p (a b)")))
                V.tensor_scalar(fve[:, i:i + 1], fmv[:, i, 1:2], EPS, None, ALU.add).then_inc(s_fve, 1)

            dve.wait_ge(s_fg, 32)
            for t in range(NT):
                final_stats(t)
                dve.wait_ge(s_fve, t + 1)
                V.scalar_tensor_tensor(out=f_rows[:, t, :], in0=f_rows[:, t, :], scalar=fmv[:, t, 0:1], in1=g_2[:],
                                       op0=ALU.subtract, op1=ALU.mult).then_inc(s_fm, 1)

        @block.gpsimd
        def _(pool):
            G = nc.gpsimd
            ch = Chain(pool, s_pool_c)
            ch.link(G.memset(half[:], -0.5))
            ch.link(G.memset(ident[:], 0.0))
            G.affine_select(out=ident[:], in_=ident[:], compare_op=ALU.not_equal, fill=1.0, base=0,
                            pattern=[[-1, P]], channel_multiplier=1).then_inc(s_cset, 1)
            G.memset(vhist[:], 0.0)
            G.memset(zhist[:], 0.0)
            G.iota(edge[:], pattern=[[0, NG], [1, HIST]], base=1, channel_multiplier=0,
                   allow_small_or_imprecise_dtypes=True).then_inc(s_cset, 1)

            def inv_root(n):
                pool.wait_ge(s_ve, n + 1)
                G.tensor_tensor(rstd[:], vareps[:], half[:], ALU.pow).then_inc(s_rstd, 1)

            def tile_rows(c, t):
                return bass.ds((c * TPC + t) * P, P)

            def h_norm(c, t, n):
                inv_root(n)
                pool.wait_ge(s_h, c * TPC + t + 1)
                carry(pool, s_pool_past)
                pool.dma_start(h0_dram[tile_rows(c, t), :], hrow[:, t % 2, :]).then_inc(s_h0out[t], 16)

            def x_load(c, t):
                if t >= 2:
                    pool.wait_ge(s_tr, (c * TPC + t - 1) * 2)
                    pool.wait_ge(s_h0out[t - 2], c * 16)
                elif not (isinstance(c, int) and c == 1):
                    pool.wait_ge(s_tr, (c * TPC + t - 1) * 2)
                    pool.wait_ge(s_h0out[t + 2], (c - 1) * 16)
                carry(pool, s_pool_past)
                pool.dma_start(hrow[:, t % 2, :], x_rows[tile_rows(c, t), :]).then_inc(s_x[t % 2], 16)

            def h1_norm(c, t, n):
                inv_root(n)
                pool.wait_ge(s_h1, c * TPC + t + 1)
                carry(pool, s_pool_past)
                pool.dma_start(h1_dram[tile_rows(c, t), :], hres[:, t, :]).then_inc(s_h1out[t], 16)

            def chunk(c, first, last):
                n = TPC if first else (c - 1) * 8 + 2 * TPC
                if not last:
                    x_load(c + 1, 0)
                    x_load(c + 1, 1)
                if not first:
                    for t in range(TPC):
                        h1_norm(c - 1, t, n)
                        n = n + 1
                if not last:
                    h_norm(c + 1, 0, n)
                    h_norm(c + 1, 1, n + 1)
                    x_load(c + 1, 2)
                    x_load(c + 1, 3)
                    h_norm(c + 1, 2, n + 2)
                    h_norm(c + 1, 3, n + 3)

            for t in range(TPC):
                inv_root(t)
            with nc.allow_non_contiguous_dma(reason="small vectors by channel"):
                pool.dma_start(cw[:], conv_w[0].rearrange("w (g p) -> p w g", p=P)).then_inc(s_const, 16)
                pool.dma_start(cb[:], conv_b[0].rearrange("(g p) -> p g", p=P)).then_inc(s_const, 16)
                pool.dma_start(ps[:], pool_scale[0].rearrange("(g p) -> p g", p=P)).then_inc(s_const, 16)
            pool.dma_start(pw_raw, pool_w[0].rearrange("g c d -> c g d")).then_inc(s_const, 16)
            pool.dma_start(wr[:], w_router.rearrange("(k p) e -> p k e", p=P)).then_inc(s_const, 16)
            pool.dma_start(g_1[:], bc(ln1_g[0])).then_inc(s_const, 16)
            pool.dma_start(b_1[:], bc(ln1_b[0])).then_inc(s_const, 16)
            chunk(0, True, False)
            with pool.Fori(1, NCH - 1) as c:
                chunk(c, False, False)
            chunk(NCH - 1, False, True)
            for t in range(TPC):
                h1_norm(NCH - 1, t, 8 * NCH - TPC + t)
            pool.wait_ge(s_out, NCH * 2 * TPC)
            pool.dma_start(bias_bc[:], bc(router_bias)).then_inc(s_rin, 16)
            G.iota(iota_e[:], pattern=[[1, NE]], base=0, channel_multiplier=0, allow_small_or_imprecise_dtypes=True)
            G.iota(iota_k[:], pattern=[[P, NE]], base=0, channel_multiplier=0, allow_small_or_imprecise_dtypes=True)
            a = ch.mark(G.memset(upper[:], 1.0))
            G.memset(ones[:], 1.0).then_inc(s_rset, 1)
            ch.need(a)
            G.affine_select(out=upper[:], in_=upper[:], compare_op=ALU.is_gt, fill=0.0, base=0,
                            pattern=[[1, P]], channel_multiplier=-1).then_inc(s_rset, 1)
            G.iota(iota_p[:], pattern=[[1, P]], base=0, channel_multiplier=0, allow_small_or_imprecise_dtypes=True)
            G.iota(iota_b[:], pattern=[[1, NBP + 1]], base=0, channel_multiplier=0,
                   allow_small_or_imprecise_dtypes=True).then_inc(s_rset, 1)
            G.iota(carries[:], pattern=[[0, NE], [1, NT]], base=0, channel_multiplier=0,
                   allow_small_or_imprecise_dtypes=True).then_inc(s_rset, 1)
            pool.wait_ge(s_rset, 4)
            G.tensor_scalar(carries[:], carries[:], 1.0, None, ALU.min).then_inc(s_rset, 1)
            G.iota(dest[:], pattern=[[0, 2], [P, NT]], base=1, channel_multiplier=1,
                   allow_small_or_imprecise_dtypes=True).then_inc(s_rset, 1)

            for j in range(EU):
                pool.wait_ge(s_hi, MU + j + 1)
                G.tensor_tensor(ring_lo[:, j:j + 1, :], staged(j), ring_hi[:, j:j + 1, :].bitcast(F32),
                                ALU.subtract).then_inc(s_lo, 1)

            pool.wait_ge(s_lst, 1)
            G.memset(xg[:], 0.0).then_inc(s_zero, 1)
            pool.wait_ge(s_tab, 1)
            nb = pool.value_load(nblocks[0:1, 0:1], min_val=NE, max_val=NB)

            def gather(b):
                G.tensor_copy(gat_now[:], token[:, bass.ds(b, 1)]).then_inc(s_gn, 1)
                pool.wait_ge(s_gn, b + 1)
                carry(pool, s_pool_past)
                G.indirect_dma_start(xg[:], None, h1_dram, bass.IndirectOffsetOnAxis(ap=gat_now[:, 0:1], axis=0),
                                     bounds_check=SEQ - 1, oob_is_err=False).then_inc(s_gat, 16)

            def put(b):
                pool.wait_ge(s_y, b + 2)
                G.tensor_copy(put_now[:], token[:, bass.ds(b, 1)]).then_inc(s_pn, 1)
                pool.wait_ge(s_pn, b + 1)
                carry(pool, s_pool_past)
                G.indirect_dma_start(sum_dram, bass.IndirectOffsetOnAxis(ap=put_now[:, 0:1], axis=0), yrow[:], None,
                                     bounds_check=SEQ - 1, oob_is_err=False, compute_op=ALU.add).then_inc(s_put, 16)

            def put_done(puts):
                pool.wait_ge(s_put, puts * 16)
                pool.sem_inc(s_yfree, 1)

            pool.sem_inc(s_yfree, 1)
            pool.sem_inc(s_y, 1)
            pool.wait_ge(s_zero, 1)
            gather(0)
            pool.wait_ge(s_gat, 16)
            pool.wait_ge(s_xt, 2)
            gather(1)
            nb1 = pool.value_load(nblocks[0:1, 1:2], min_val=NE - 1, max_val=NB - 1)
            nb2 = pool.value_load(nblocks[0:1, 2:3], min_val=NE - 2, max_val=NB - 2)
            pool.wait_ge(s_xt, 4)
            pool.wait_ge(s_gat, 32)
            gather(2)
            pool.wait_ge(s_xt, 6)
            pool.wait_ge(s_gat, 48)
            gather(3)
            put(0)
            with pool.Fori(2, nb1) as b:
                pool.wait_ge(s_xt, b * 2 + 4)
                pool.wait_ge(s_gat, b * 16 + 32)
                gather(b + 2)
                put_done(b - 1)
                put(b - 1)
            put_done(nb2)
            put(nb2)
            put_done(nb1)
            put(nb1)
            pool.wait_ge(s_gat, nb * 16 + 16)
            pool.wait_ge(s_put, nb * 16)
            pool.sem_inc(s_allput, 1)

            def final_root(t):
                i = t
                pool.wait_ge(s_fve, t + 1)
                G.tensor_tensor(frstd[:, i:i + 1], fve[:, i:i + 1], half[:], ALU.pow).then_inc(s_fr, 1)

            def final_bias(t):
                i = t
                pool.wait_ge(s_fn, t + 1)
                G.tensor_tensor(f_rows[:, i, :], f_rows[:, i, :], b_2[:], ALU.add).then_inc(s_fo, 1)

            for t in range(NT + 1):
                if t < NT:
                    final_root(t)
                if t >= 1:
                    final_bias(t - 1)


_INS = ["x", "ln_in_g", "ln_in_b", "w_in", "pool_w", "pool_scale", "conv_w", "conv_b", "w_out", "ln1_g", "ln1_b",
        "w_router", "router_bias", "exp_w1", "exp_w3", "exp_w2", "ln2_g", "ln2_b"]


def kernel(**inputs):
    from concourse import bacc
    from concourse.bass_utils import run_bass_kernel_spmd

    nc = bacc.Bacc("TRN2", target_bir_lowering=False, num_devices=1)
    arrays, args = {}, []
    for name in _INS:
        a = np.ascontiguousarray(inputs[name])
        arrays[f"in_{name}"] = a
        args.append(nc.dram_tensor(f"in_{name}", a.shape, mybir.dt.from_np(a.dtype), kind="ExternalInput").ap())
    out = nc.dram_tensor("out", (1, SEQ, D), F32, kind="ExternalOutput").ap()
    build(nc, *args, out)
    r = run_bass_kernel_spmd(nc, [arrays], core_ids=[0])
    return r.results[0]["out"]
```
